# Optimizing a Trainium2 kernel written in Bass

```python
import jax, jax.numpy as jnp
from jax import lax
import numpy as np

D_MODEL = 1024
BATCH = 1
SEQ = 128
DEPTH = 1
DEC_BATCH = 1
DEC_SEQ = 512
PAST_LEN = 128

GRID_W = 64
EPS = 1e-6
MLA_HEADS = 8
MLA_NOPE = 64
MLA_ROPE = 32
MLA_V = 64
Q_LORA = 256
KV_LORA = 128
ROPE_BASE = 10000.0
ATTN_BLOCK = 128
RET_HEADS = 4
RET_DK = 128
RET_DV = 128
RET_CHUNK = 64
MIX_A = MLA_HEADS * MLA_V
MIX_B = RET_HEADS * RET_DV
IN_SIZES = (Q_LORA, KV_LORA, MLA_ROPE, RET_HEADS * RET_DK, RET_HEADS * RET_DK, MIX_B, MIX_B, D_MODEL, D_MODEL)
D_IN = Q_LORA + KV_LORA + MLA_ROPE + 2 * RET_HEADS * RET_DK + 2 * MIX_B + 2 * D_MODEL
PEER_HEADS = 8
PEER_DQ = 256
N_KEYS = 128
N_EXPERTS = N_KEYS * N_KEYS
PEER_TOPK = 16
PEER_BLOCK = 128

kernel_name = 'hybrid_mla_retention_peer_diffusion_step'

def _split(a, sizes):
    out = []
    start = 0
    for s in sizes:
        out.append(a[..., start:start + s])
        start += s
    return out

def _rmsnorm(x, g):
    xf = x.astype(jnp.float32)
    xf = xf * lax.rsqrt(jnp.mean(xf * xf, axis=-1, keepdims=True) + EPS)
    return xf.astype(x.dtype) * g

def _modulate(h, shift, scale):
    return h * (1 + scale) + shift

def _rope_2d(x):
    T = x.shape[1]
    rows = T // GRID_W
    row = jnp.repeat(jnp.arange(rows, dtype=jnp.float32), GRID_W)
    col = jnp.tile(jnp.arange(GRID_W, dtype=jnp.float32), rows)
    nf = MLA_ROPE // 4
    freqs = jnp.power(ROPE_BASE, -jnp.arange(nf, dtype=jnp.float32) / nf)
    ang = jnp.concatenate([row[:, None] * freqs, col[:, None] * freqs], axis=-1)
    ang = ang.reshape((T,) + (1,) * (x.ndim - 3) + (MLA_ROPE // 2,))
    cos = jnp.cos(ang).astype(x.dtype)
    sin = jnp.sin(ang).astype(x.dtype)
    x1, x2 = x[..., :MLA_ROPE // 2], x[..., MLA_ROPE // 2:]
    return jnp.concatenate([x1 * cos - x2 * sin, x1 * sin + x2 * cos], axis=-1)

def _project(h, w_in, q_norm, kv_norm, w_uq):
    B, T, _ = h.shape
    cq, ckv, kr, rq, rk, rv, rg, ga, gb = _split(h @ w_in, IN_SIZES)
    q = (_rmsnorm(cq, q_norm) @ w_uq).reshape(B, T, MLA_HEADS, MLA_NOPE + MLA_ROPE)
    qn, qr = q[..., :MLA_NOPE], q[..., MLA_NOPE:]
    ckv = _rmsnorm(ckv, kv_norm)
    rq = rq.reshape(B, T, RET_HEADS, RET_DK)
    rk = rk.reshape(B, T, RET_HEADS, RET_DK) * (RET_DK ** -0.5)
    rv = rv.reshape(B, T, RET_HEADS, RET_DV)
    return qn, qr, ckv, kr, rq, rk, rv, rg, ga, gb

def _expand_kv(ckv, w_ukv):
    B, T, _ = ckv.shape
    kv = (ckv @ w_ukv).reshape(B, T, MLA_HEADS, MLA_NOPE + MLA_V)
    return kv[..., :MLA_NOPE], kv[..., MLA_NOPE:]

def _mla_attend(q_nope, q_rope, k_nope, k_rope, v):
    B, Tq, H, _ = q_nope.shape
    nb = Tq // ATTN_BLOCK
    scale = (MLA_NOPE + MLA_ROPE) ** -0.5

    def block(qs):
        qn, qr = qs
        s = jnp.einsum('bqhd,bkhd->bhqk', qn, k_nope) + jnp.einsum('bqhr,bkr->bhqk', qr, k_rope)
        p = jax.nn.softmax(s.astype(jnp.float32) * scale, axis=-1).astype(v.dtype)
        return jnp.einsum('bhqk,bkhd->bqhd', p, v)

    qb = lambda a: jnp.moveaxis(a.reshape(B, nb, ATTN_BLOCK, H, a.shape[-1]), 1, 0)
    out = lax.map(block, (qb(q_nope), qb(q_rope)))
    return jnp.moveaxis(out, 0, 1).reshape(B, Tq, H * MLA_V)

def _retention_dir(q, k, v, decay_logit, s0):
    B, T, H, dk = q.shape
    dv = v.shape[-1]
    C = RET_CHUNK
    n = T // C
    lg = jax.nn.log_sigmoid(decay_logit.astype(jnp.float32))[:, None]
    idx = jnp.arange(C, dtype=jnp.float32)
    diff = idx[:, None] - idx[None, :]
    dmat = jnp.where(diff >= 0, jnp.exp(lg[:, :, None] * jnp.maximum(diff, 0.0)), 0.0)
    q_dec = jnp.exp(lg * (idx + 1.0)).T
    k_dec = jnp.exp(lg * (C - 1.0 - idx)).T
    c_dec = jnp.exp(lg[:, 0] * C)
    chunks = lambda a: jnp.moveaxis(a.astype(jnp.float32).reshape(B, n, C, H, a.shape[-1]), 1, 0)

    def step(S, inp):
        qc, kc, vc = inp
        sc = jnp.einsum('bihd,bjhd->bhij', qc, kc) * dmat
        intra = jnp.einsum('bhij,bjhe->bihe', sc, vc)
        cross = jnp.einsum('bihd,bhde->bihe', qc * q_dec[None, :, :, None], S)
        S_new = S * c_dec[None, :, None, None] + jnp.einsum('bjhd,bjhe->bhde', kc * k_dec[None, :, :, None], vc)
        return S_new, intra + cross

    S_fin, out = lax.scan(step, s0.astype(jnp.float32), (chunks(q), chunks(k), chunks(v)))
    out = jnp.moveaxis(out, 0, 1).reshape(B, T, H, dv)
    return out, S_fin.astype(s0.dtype)

def _retention(rq, rk, rv, rg, logit_f, logit_b, s0_f, s0_b, gn):
    y_f, s_f = _retention_dir(rq, rk, rv, logit_f, s0_f)
    y_b, s_b = _retention_dir(jnp.flip(rq, 1), jnp.flip(rk, 1), jnp.flip(rv, 1), logit_b, s0_b)
    y = y_f + jnp.flip(y_b, 1)
    mu = jnp.mean(y, axis=-1, keepdims=True)
    var = jnp.mean(jnp.square(y - mu), axis=-1, keepdims=True)
    y = ((y - mu) * lax.rsqrt(var + EPS)).astype(rv.dtype)
    B, T = y.shape[0], y.shape[1]
    y = y.reshape(B, T, MIX_B) * gn
    return jax.nn.silu(rg) * y, s_f, s_b

def _merge(attn, ret, ga, gb, w_up_a, w_up_b, w_o):
    return (jax.nn.sigmoid(ga) * (attn @ w_up_a) + jax.nn.sigmoid(gb) * (ret @ w_up_b)) @ w_o

def _peer(h, wq, keys1, keys2, u_tab, v_tab):
    B, T, D = h.shape
    xb_all = h.reshape(-1, PEER_BLOCK, D)

    def block(xb):
        q = (xb @ wq).reshape(PEER_BLOCK, PEER_HEADS, PEER_DQ)
        q1, q2 = q[..., :PEER_DQ // 2], q[..., PEER_DQ // 2:]
        s1 = jnp.einsum('nhd,hkd->nhk', q1, keys1).astype(jnp.float32)
        s2 = jnp.einsum('nhd,hkd->nhk', q2, keys2).astype(jnp.float32)
        v1, i1 = lax.top_k(s1, PEER_TOPK)
        v2, i2 = lax.top_k(s2, PEER_TOPK)
        cand = (v1[..., :, None] + v2[..., None, :]).reshape(PEER_BLOCK, PEER_HEADS, PEER_TOPK * PEER_TOPK)
        vals, ci = lax.top_k(cand, PEER_TOPK)
        e = jnp.take_along_axis(i1, ci // PEER_TOPK, axis=-1) * N_KEYS + jnp.take_along_axis(i2, ci % PEER_TOPK, axis=-1)
        g = jax.nn.softmax(vals, axis=-1).astype(xb.dtype)
        a = jax.nn.gelu(jnp.einsum('nd,nhkd->nhk', xb, u_tab[e]))
        return jnp.einsum('nhk,nhkd->nd', g * a, v_tab[e])

    return lax.map(block, xb_all).reshape(B, T, D)

def setup_inputs(seed: int = 0) -> dict:
    key = jax.random.key(seed)
    ks = iter(jax.random.split(key, 40))
    nrm = lambda shape, s: s * jax.random.normal(next(ks), shape, jnp.float32)
    ones = lambda shape: 1.0 + nrm(shape, 0.01)
    base_logit = jnp.log(jnp.exp2(5.0 + jnp.arange(RET_HEADS, dtype=jnp.float32)) - 1.0)
    return {
        'x_prompt': nrm((BATCH, SEQ, D_MODEL), 1.0),
        'x_sample': nrm((DEC_BATCH, DEC_SEQ, D_MODEL), 1.0),
        'c': nrm((DEC_BATCH, D_MODEL), 1.0),
        'cache_ckv': nrm((DEC_BATCH, DEPTH, PAST_LEN, KV_LORA), 1.0),
        'cache_krope': nrm((DEC_BATCH, DEPTH, PAST_LEN, MLA_ROPE), 1.0),
        'state_ret_fwd': nrm((DEC_BATCH, DEPTH, RET_HEADS, RET_DK, RET_DV), 0.5),
        'state_ret_bwd': nrm((DEC_BATCH, DEPTH, RET_HEADS, RET_DK, RET_DV), 0.5),
        'c_ctx': nrm((D_MODEL,), 1.0),
        'w_mod': nrm((DEPTH, D_MODEL, 6 * D_MODEL), 0.5 * D_MODEL ** -0.5),
        'b_mod': nrm((DEPTH, 6 * D_MODEL), 0.01),
        'norm_mix': ones((DEPTH, D_MODEL)),
        'norm_ffn': ones((DEPTH, D_MODEL)),
        'norm_final': ones((D_MODEL,)),
        'w_in': nrm((DEPTH, D_MODEL, D_IN), D_MODEL ** -0.5),
        'q_norm': ones((DEPTH, Q_LORA)),
        'kv_norm': ones((DEPTH, KV_LORA)),
        'w_uq': nrm((DEPTH, Q_LORA, MLA_HEADS * (MLA_NOPE + MLA_ROPE)), Q_LORA ** -0.5),
        'w_ukv': nrm((DEPTH, KV_LORA, MLA_HEADS * (MLA_NOPE + MLA_V)), KV_LORA ** -0.5),
        'ret_logit_fwd': base_logit[None, :] + nrm((DEPTH, RET_HEADS), 0.01),
        'ret_logit_bwd': base_logit[None, :] + nrm((DEPTH, RET_HEADS), 0.01),
        'ret_gn': ones((DEPTH, MIX_B)),
        'w_up_a': nrm((DEPTH, MIX_A, D_MODEL), MIX_A ** -0.5),
        'w_up_b': nrm((DEPTH, MIX_B, D_MODEL), MIX_B ** -0.5),
        'w_o': nrm((DEPTH, D_MODEL, D_MODEL), D_MODEL ** -0.5),
        'peer_wq': nrm((DEPTH, D_MODEL, PEER_HEADS * PEER_DQ), D_MODEL ** -0.5),
        'peer_keys1': nrm((DEPTH, PEER_HEADS, N_KEYS, PEER_DQ // 2), (PEER_DQ // 2) ** -0.5),
        'peer_keys2': nrm((DEPTH, PEER_HEADS, N_KEYS, PEER_DQ // 2), (PEER_DQ // 2) ** -0.5),
        'peer_u': nrm((DEPTH, N_EXPERTS, D_MODEL), D_MODEL ** -0.5),
        'peer_v': nrm((DEPTH, N_EXPERTS, D_MODEL), 0.1),
    }

def reference(x_prompt, x_sample, c, cache_ckv, cache_krope, state_ret_fwd, state_ret_bwd, c_ctx,
              w_mod, b_mod, norm_mix, norm_ffn, norm_final, w_in, q_norm, kv_norm, w_uq, w_ukv,
              ret_logit_fwd, ret_logit_bwd, ret_gn, w_up_a, w_up_b, w_o,
              peer_wq, peer_keys1, peer_keys2, peer_u, peer_v):
    xp, xs = x_prompt, x_sample
    new_ckv, new_kr, new_sf, new_sb = [], [], [], []
    for l in range(DEPTH):
        mod_c = jax.nn.silu(c_ctx) @ w_mod[l] + b_mod[l]
        mod_s = (jax.nn.silu(c) @ w_mod[l] + b_mod[l])[:, None, :]
        sh1c, sc1c, g1c, sh2c, sc2c, g2c = _split(mod_c, (D_MODEL,) * 6)
        sh1s, sc1s, g1s, sh2s, sc2s, g2s = _split(mod_s, (D_MODEL,) * 6)

        h = _modulate(_rmsnorm(xp, norm_mix[l]), sh1c, sc1c)
        qn, qr, ckv, kr, rq, rk, rv, rg, ga, gb = _project(h, w_in[l], q_norm[l], kv_norm[l], w_uq[l])
        kn, v = _expand_kv(ckv, w_ukv[l])
        attn = _mla_attend(qn, qr, kn, kr, v)
        zero = jnp.zeros((xp.shape[0], RET_HEADS, RET_DK, RET_DV), xp.dtype)
        ret, sf, sb = _retention(rq, rk, rv, rg, ret_logit_fwd[l], ret_logit_bwd[l], zero, zero, ret_gn[l])
        xp = xp + g1c * _merge(attn, ret, ga, gb, w_up_a[l], w_up_b[l], w_o[l])
        h = _modulate(_rmsnorm(xp, norm_ffn[l]), sh2c, sc2c)
        xp = xp + g2c * _peer(h, peer_wq[l], peer_keys1[l], peer_keys2[l], peer_u[l], peer_v[l])
        new_ckv.append(ckv)
        new_kr.append(kr)
        new_sf.append(sf)
        new_sb.append(sb)

        h = _modulate(_rmsnorm(xs, norm_mix[l]), sh1s, sc1s)
        qn, qr, ckv_s, kr_s, rq, rk, rv, rg, ga, gb = _project(h, w_in[l], q_norm[l], kv_norm[l], w_uq[l])
        qr = _rope_2d(qr)
        kr_s = _rope_2d(kr_s)
        ckv_all = jnp.concatenate([ckv_s, cache_ckv[:, l]], axis=1)
        kr_all = jnp.concatenate([kr_s, cache_krope[:, l]], axis=1)
        kn, v = _expand_kv(ckv_all, w_ukv[l])
        attn = _mla_attend(qn, qr, kn, kr_all, v)
        ret, _, _ = _retention(rq, rk, rv, rg, ret_logit_fwd[l], ret_logit_bwd[l],
                               state_ret_fwd[:, l], state_ret_bwd[:, l], ret_gn[l])
        xs = xs + g1s * _merge(attn, ret, ga, gb, w_up_a[l], w_up_b[l], w_o[l])
        h = _modulate(_rmsnorm(xs, norm_ffn[l]), sh2s, sc2s)
        xs = xs + g2s * _peer(h, peer_wq[l], peer_keys1[l], peer_keys2[l], peer_u[l], peer_v[l])

    y_prompt = _rmsnorm(xp, norm_final)
    y_sample = _rmsnorm(xs, norm_final)
    return (y_prompt, y_sample, jnp.stack(new_ckv, axis=1), jnp.stack(new_kr, axis=1),
            jnp.stack(new_sf, axis=1), jnp.stack(new_sb, axis=1))


_drawn_inputs = setup_inputs


def setup_inputs(seed=0):
    import zlib

    import numpy as np

    out = dict(_drawn_inputs(seed))
    spreads = {}
    factors = {'cache_ckv': 8.0,
     'cache_krope': 8.0,
     'state_ret_fwd': 4.176,
     'state_ret_bwd': 4.196,
     'norm_mix': 5.004,
     'norm_ffn': 8.0,
     'norm_final': 5.762,
     'q_norm': 8.0,
     'kv_norm': 5.696,
     'w_uq': 2.716,
     'ret_gn': 8.0,
     'peer_wq': 3.31,
     'peer_keys1': 3.376,
     'peer_keys2': 3.376,
     'peer_u': 3.725,
     'peer_v': 3.316}
    for name, (base, spread) in spreads.items():
        noise = np.random.default_rng([zlib.crc32(name.encode()), seed]).standard_normal(out[name].shape)
        drawn = base * np.exp(spread * noise) if base else spread * noise
        out[name] = __import__('jax').numpy.asarray(drawn.astype(out[name].dtype))
    for name, factor in factors.items():
        out[name] = (out[name] * factor).astype(out[name].dtype)
    return out
```

```python
from contextlib import ExitStack

import numpy as np

import concourse.bass as bass
from concourse import mybir

F32 = mybir.dt.float32
F32R = mybir.dt.float32r
U32 = mybir.dt.uint32
ACT = mybir.ActivationFunctionType
ALU = mybir.AluOpType
AX = mybir.AxisListType

P = 128
D = 1024
KC = D // P
NCTX, NLAT = 128, 512
N = NCTX + NLAT
NT = N // P
NH2 = N // 2
PAST = 128
NALL = N + PAST
EPS = 1e-6
HEADS, NOPE, ROPE, VD = 8, 64, 32, 64
QK = NOPE + ROPE
ATT_SCALE = QK ** -0.5
RH, DK = 4, 128
RET_SCALE = DK ** -0.5
PH, TOPK = 8, 16
PICKS = PH * TOPK
NK = 128
NMOD = 6 * KC
M_CQ, M_CKV, M_KR, M_RQ, M_RK, M_RV, M_RG, M_GATE, M_END = 0, 2, 3, 4, 8, 12, 16, 20, 36
GRID_W, ROPE_BASE = 64, 10000.0
LOW = -3.0e38
WB = 64
OB = 8
U_AHEAD = 24
VG = 2
VGROUPS = NK // VG
YBANKS = 5


class Sems:

    def __init__(self, nc):
        self.nc, self.made = nc, {}

    def __call__(self, name):
        if name not in self.made:
            self.made[name] = self.nc.alloc_semaphore(name=name)
        return self.made[name]

    def clear(self):
        self.nc.all_engine_barrier()
        self.nc.clear_and_free_semaphores(list(self.made.values()))
        self.nc.all_engine_barrier()
        self.made = {}


def run(eng, first, end, step):
    step(first)
    with eng.Fori(first + 1, end) as i:
        step(i)


class Chain:

    def __init__(self, eng, sem):
        self.eng, self.sem, self.n = eng, sem, 0

    def __call__(self, ins):
        self.n += 1
        ins.then_inc(self.sem, 1)
        self.eng.wait_ge(self.sem, self.n)


def build(nc, a, outs):
    y_prompt, y_sample, new_ckv, new_kr, new_sf, new_sb = outs
    gates_d = nc.dram_tensor("gates_scratch", (16, P, N), F32, kind="Internal").ap()
    scores_d = nc.dram_tensor("scores_scratch", (NT, P, 16 * NK), F32, kind="Internal").ap()
    x2_d = nc.dram_tensor("x2_scratch", (NT, P, D), F32, kind="Internal").ap()
    act_d = nc.dram_tensor("act_scratch", (NK, P, N), F32, kind="Internal").ap()
    wgt_d = nc.dram_tensor("wgt_scratch", (P, N // WB, NK * WB), F32, kind="Internal").ap()

    with ExitStack() as top:
        s = Sems(nc)

        def sb(ctx, name, shape, dt=F32):
            return ctx.enter_context(nc.sbuf_tensor(name, shape, dt))

        def pb(ctx, name, shape, dt=F32):
            return ctx.enter_context(nc.psum_tensor(name, shape, dt))

        mod = sb(top, "mod", [P, NMOD, 2])
        cols = sb(top, "cols", [P, 40])
        ident = sb(top, "ident", [P, P])
        h_hi = sb(top, "h_hi", [P, KC, N], F32R)
        h_lo = sb(top, "h_lo", [P, KC, N], F32R)

        class Linear:

            def __init__(self, ctx, tag, w_dram, count, banks):
                self.tag, self.w, self.count, self.ps = tag, w_dram, count, banks
                self.raw = [sb(ctx, f"{tag}_raw{b}", [P, KC, P]) for b in (0, 1)]
                self.hi = [sb(ctx, f"{tag}_hi{b}", [P, KC, P], F32R) for b in (0, 1)]
                self.lo = [sb(ctx, f"{tag}_lo{b}", [P, KC, P], F32R) for b in (0, 1)]

            def sem(self, what, b):
                return s(f"{self.tag}_{what}{b}")

            def load(self, sp, pair, b):
                sp.wait_ge(self.sem("split", b), pair)
                sp.dma_start(self.raw[b][:, :, :].rearrange("p k m -> p (k m)"),
                             self.w[bass.ds(2 * pair + b, 1)].rearrange("o p m -> p (o m)")
                             ).then_inc(self.sem("loaded", b), 16)

            def head(self, act, pair, b):
                act.wait_ge(self.sem("loaded", b), 16 * pair + 16)
                act.wait_ge(self.sem("product", b), pair)
                nc.scalar.activation(self.hi[b][:], self.raw[b][:], ACT.Copy).then_inc(self.sem("head", b), 1)

            def rest(self, pool, pair, b):
                pool.wait_ge(self.sem("head", b), pair + 1)
                nc.gpsimd.tensor_tensor(self.lo[b][:], self.raw[b][:], self.hi[b][:].bitcast(F32),
                                        ALU.subtract).then_inc(self.sem("split", b), 1)

            def product(self, pe, pair, b, groups=((0, KC),)):
                pe.wait_ge(self.sem("split", b), pair + 1)
                pe.wait_ge(self.sem("evac", b), pair)
                for g, (k0, k1) in enumerate(groups):
                    for half in (0, 1):
                        cs = slice(half * NH2, half * NH2 + NH2)
                        out = self.ps[b][:, 2 * g + half, 0:NH2]
                        for kc in range(k0, k1):
                            nc.tensor.matmul(out, self.hi[b][:, kc, :], h_hi[:, kc, cs],
                                             start=(kc == k0), stop=False)
                            nc.tensor.matmul(out, self.hi[b][:, kc, :], h_lo[:, kc, cs],
                                             start=False, stop=False)
                            last = nc.tensor.matmul(out, self.lo[b][:, kc, :], h_hi[:, kc, cs],
                                                    start=False, stop=(kc == k1 - 1))
                last.then_inc(self.sem("product", b), 1)

            def wait_out(self, eng, pair, b):
                eng.wait_ge(self.sem("product", b), pair + 1)

            def out(self, b, g=0):
                return self.ps[b][:, 2 * g:2 * g + 2, 0:NH2]

        def halves(ap):
            return ap.rearrange("p (h n) -> p h n", h=2)

        def rstd_ops(dve, link, tag, mean_sq, var_out, var, root, r, t):
            nc.vector.tensor_scalar(var_out, mean_sq, EPS, None, ALU.add).then_inc(s(tag + "_var"), 1)
            dve.wait_ge(s(tag + "_root"), 1)
            link(nc.vector.reciprocal(r, root))
            link(nc.vector.tensor_tensor(t, r, r, ALU.mult))
            link(nc.vector.tensor_tensor(t, t, var, ALU.mult))
            link(nc.vector.tensor_scalar(t, t, -0.5, 1.5, ALU.mult, ALU.add))
            link(nc.vector.tensor_tensor(r, r, t, ALU.mult))

        C_MIX, C_FFN, C_QN, C_KVN, C_GN, C_LOG = 0, 8, 16, 18, 19, 23

        with ExitStack() as mixer:
            x_t = sb(mixer, "x_t", [P, KC, N])
            act_buf = sb(mixer, "act_buf", [P, KC, N])
            gscale = sb(mixer, "gscale", [P, KC, 2])

            def norm_pe(pe, tag, src, inv_in, ps, sq_sem):
                for kc in range(KC):
                    pe.wait_ge(s(sq_sem), kc + 1)
                    for half in (0, 1):
                        last = nc.tensor.matmul(ps[:, half, 0:NH2], inv_in[:],
                                                src[:, kc, half * NH2:half * NH2 + NH2],
                                                start=(kc == 0), stop=(kc == KC - 1))
                last.then_inc(s(tag + "_meansq"), 1)

            def norm_dve(dve, link, tag, ps, wrk, c_norm, m_shift, m_scale):
                var, root, r, t = wrk
                for g in (0, 1):
                    link(nc.vector.scalar_tensor_tensor(
                        out=gscale[:, :, g], in0=mod[:, m_scale:m_scale + KC, g], scalar=1.0,
                        in1=cols[:, c_norm:c_norm + KC], op0=ALU.add, op1=ALU.mult))
                dve.wait_ge(s(tag + "_meansq"), 1)

                rstd_ops(dve, link, tag, ps[:, :, 0:NH2], halves(var[:, :]), var[:, :], root[:, :], r[:, :], t[:, :])
                for kc in range(KC):
                    link(nc.vector.tensor_tensor(act_buf[:, kc, :], x_t[:, kc, :], r[:, :], ALU.mult))
                    for g, cs in ((0, slice(0, NCTX)), (1, slice(NCTX, N))):
                        ins = nc.vector.tensor_scalar(
                            act_buf[:, kc, cs], act_buf[:, kc, cs], gscale[:, kc, g:g + 1],
                            mod[:, m_shift + kc, g:g + 1], ALU.mult, ALU.add)
                        ins.then_inc(s(tag + "_h"), 1)
                for kc in range(KC):
                    dve.wait_ge(s(tag + "_hi"), kc + 1)
                    nc.vector.tensor_tensor(h_lo[:, kc, :], act_buf[:, kc, :],
                                            h_hi[:, kc, :].bitcast(F32), ALU.subtract
                                            ).then_inc(s(tag + "_split"), 1)

            def norm_act(act, tag, wrk):
                var, root, r, t = wrk
                act.wait_ge(s(tag + "_var"), 1)
                nc.scalar.activation(root[:, :], var[:, :], ACT.Sqrt).then_inc(s(tag + "_root"), 1)
                for kc in range(KC):
                    act.wait_ge(s(tag + "_h"), 2 * kc + 2)
                    nc.scalar.activation(h_hi[:, kc, :], act_buf[:, kc, :], ACT.Copy
                                         ).then_inc(s(tag + "_hi"), 1)

            with ExitStack() as keep:
                proj = sb(keep, "proj", [P, M_GATE, N])

                with ExitStack() as c1:
                    wm = [sb(c1, f"wm{b}", [P, KC, P]) for b in (0, 1)]
                    cvec = sb(c1, "cvec", [P, KC, 2])
                    csil = sb(c1, "csil", [P, KC, 2])
                    bmod = sb(c1, "bmod", [P, NMOD])
                    inv_d = sb(c1, "inv_d", [P, P])
                    wrk = [sb(c1, f"n1_{n}", [P, N]) for n in ("var", "root", "r", "t")]
                    gate = [sb(c1, f"gate{b}", [P, N]) for b in (0, 1)]
                    ps_mod = pb(c1, "ps_mod", [P, NMOD, 2])
                    ps_n = pb(c1, "ps_n", [P, 2, 512])
                    banks = [pb(c1, f"win_ps{b}", [P, 2, 512]) for b in (0, 1)]
                    lin = Linear(c1, "win", a["w_in"], M_END, banks)
                    npair = M_END // 2
                    gpair = M_GATE // 2
                    block = c1.enter_context(nc.Block())

                    @block.sync
                    def _(sp):
                        for dst, name in ((cvec[:], "cvec"), (bmod[:], "bmod"), (cols[:], "cols"),
                                          (x_t[:], "x_t"), (ident[:], "ident"),
                                          (inv_d[:], "inv_d")):
                            sp.dma_start(dst, a[name]).then_inc(s("ld_" + name), 16)
                        def step(i):
                            for b in (0, 1):
                                sp.wait_ge(s(f"wm_used{b}"), i)
                                sp.dma_start(wm[b][:, :, :].rearrange("p k m -> p (k m)"),
                                             a["w_mod"][bass.ds(2 * i + b, 1)].rearrange("o p m -> p (o m)")
                                             ).then_inc(s(f"wm_ld{b}"), 16)
                        run(sp, 0, NMOD // 2, step)
                        def step(i):
                            for b in (0, 1):
                                lin.load(sp, i, b)
                        run(sp, 0, npair, step)
                        for b in (0, 1):
                            sp.wait_ge(s(f"gate_st{b}"), 16 * (npair - gpair))

                    @block.scalar
                    def _(act):
                        act.wait_ge(s("ld_cvec"), 16)
                        nc.scalar.activation(csil[:], cvec[:], ACT.Silu).then_inc(s("csil"), 1)
                        act.wait_ge(s("ld_x_t"), 16)
                        for kc in range(KC):
                            nc.scalar.activation(act_buf[:, kc, :], x_t[:, kc, :], ACT.Square
                                                 ).then_inc(s("n1_sq"), 1)
                        norm_act(act, "n1", wrk)
                        def step(i):
                            for b in (0, 1):
                                lin.head(act, i, b)
                        run(act, 0, gpair, step)
                        def step(i):
                            for b in (0, 1):
                                lin.head(act, i, b)
                                lin.wait_out(act, i, b)
                                act.wait_ge(s(f"gate_st{b}"), 16 * (i - gpair))
                                nc.scalar.activation(halves(gate[b][:, :]), lin.out(b), ACT.Sigmoid
                                                     ).then_inc(lin.sem("evac", b), 1)
                                act.wait_ge(lin.sem("evac", b), i + 1)
                                act.dma_start(gates_d[bass.ds(2 * (i - gpair) + b, 1)].rearrange("o p m -> p (o m)"),
                                              gate[b][:]).then_inc(s(f"gate_st{b}"), 16)
                        run(act, gpair, npair, step)

                    @block.gpsimd
                    def _(pool):
                        def step(i):
                            for b in (0, 1):
                                lin.rest(pool, i, b)
                        run(pool, 0, npair, step)

                    @block.vector
                    def _(dve):
                        link = Chain(dve, s("dve1"))
                        dve.wait_ge(s("wm_used1"), NMOD // 2)
                        dve.wait_ge(s("ld_bmod"), 16)
                        dve.wait_ge(s("ld_cols"), 16)
                        for g in (0, 1):
                            link(nc.vector.tensor_tensor(mod[:, :, g], ps_mod[:, :, g], bmod[:, :], ALU.add))
                        norm_dve(dve, link, "n1", ps_n, wrk, C_MIX, 0, KC)
                        def step(i):
                            for b in (0, 1):
                                lin.wait_out(dve, i, b)
                                nc.vector.tensor_copy(
                                    proj[:, bass.ds(2 * i + b, 1), :].rearrange("p o (h n) -> p (o h) n", h=2),
                                    lin.out(b)).then_inc(lin.sem("evac", b), 1)
                        run(dve, 0, gpair, step)

                    @block.tensor
                    def _(pe):
                        pe.wait_ge(s("csil"), 1)
                        pe.wait_ge(s("ld_inv_d"), 16)
                        norm_pe(pe, "n1", act_buf, inv_d, ps_n, "n1_sq")
                        def step(i):
                            for b in (0, 1):
                                pe.wait_ge(s(f"wm_ld{b}"), 16 * i + 16)
                                for kc in range(KC):
                                    last = nc.tensor.matmul(
                                        ps_mod[:, bass.ds(2 * i + b, 1), :].rearrange("p o g -> p (o g)"),
                                        wm[b][:, kc, :], csil[:, kc, :], start=(kc == 0), stop=(kc == KC - 1))
                                last.then_inc(s(f"wm_used{b}"), 1)
                        run(pe, 0, NMOD // 2, step)
                        pe.wait_ge(s("n1_split"), KC)
                        def step(i):
                            for b in (0, 1):
                                lin.product(pe, i, b)
                        run(pe, 0, npair, step)

                with ExitStack() as c2:
                    w_uq = sb(c2, "w_uq", [P, 2, D])
                    w_ukv = sb(c2, "w_ukv", [P, 2, 512])
                    cos_t = sb(c2, "cos_t", [P, NLAT])
                    sin_t = sb(c2, "sin_t", [P, NLAT])
                    inv_q = sb(c2, "inv_q", [P, P])
                    inv_k = sb(c2, "inv_k", [P, P])
                    q_h = sb(c2, "q_h", [QK, HEADS, N])
                    k_h = sb(c2, "k_h", [QK, HEADS, NALL])
                    ckv = sb(c2, "ckv", [P, NALL])
                    v_tok = sb(c2, "v_tok", [P, NALL // P, 512])
                    kr_past = sb(c2, "kr_past", [ROPE, PAST])
                    kr_new = act_buf[0:ROPE, 7, :]
                    probs = [act_buf[:, 0, :], act_buf[:, 7, :]]
                    probs_t = [act_buf[:, 1, :], act_buf[:, 2, :]]
                    stat = [sb(c2, f"stat{b}", [P, 4]) for b in (0, 1)]
                    ckv_out = act_buf[:, 3, 0:P + ROPE]
                    sq = act_buf[:, 0, :]
                    var, root, r, t = (act_buf[:, k, :] for k in (1, 2, 3, 4))
                    t1, t2 = act_buf[:, 5, 0:NLAT], act_buf[:, 6, 0:NLAT]
                    sqb = act_buf[:, 7, :]
                    ps_s = [pb(c2, f"ps_s{b}", [P, 2, 512]) for b in (0, 1)]
                    ps_t = pb(c2, "ps_t", [P, 2, 512])
                    ps_o = [pb(c2, f"ps_o{b}", [P, 512]) for b in (0, 1)]
                    units = [(qt, h) for qt in range(NT) for h in range(HEADS)]

                    def keys(qt):
                        return [0] if qt == 0 else list(range(1, NALL // P))
                    block = c2.enter_context(nc.Block())

                    @block.sync
                    def _(sp):
                        for dst, name in ((w_uq[:], "w_uq"), (w_ukv[:], "w_ukv"), (cos_t[:], "cos_t"),
                                          (sin_t[:], "sin_t"), (inv_q[:], "inv_q"), (inv_k[:], "inv_k"),
                                          (ckv[:, N:NALL], "cache_ckv_t"), (kr_past[:], "cache_kr_t")):
                            sp.dma_start(dst, a[name]).then_inc(s("ld_" + name), 16)
                        sp.wait_ge(s("ckv_out"), 2)
                        sp.dma_start(new_ckv, ckv_out[:, 0:P]).then_inc(s("st_kv"), 16)
                        sp.dma_start(new_kr, ckv_out[:, P:P + ROPE]).then_inc(s("st_kv"), 16)
                        sp.wait_ge(s("st_kv"), 32)

                    @block.scalar
                    def _(act):
                        for i, m in enumerate((M_CQ, M_CQ + 1, M_CKV)):
                            if i == 2:
                                act.wait_ge(s("cq_meansq"), 1)
                            dst = sqb if i == 1 else sq
                            nc.scalar.activation(dst, proj[:, m, :], ACT.Square).then_inc(s("lat_sq"), 1)
                            if i == 1:
                                act.wait_ge(s("cq_var"), 1)
                                nc.scalar.activation(root, var, ACT.Sqrt).then_inc(s("cq_root"), 1)
                        act.wait_ge(s("ckv_var"), 1)
                        nc.scalar.activation(root, var, ACT.Sqrt).then_inc(s("ckv_root"), 1)
                        act.wait_ge(s("kr_done"), 1)
                        act.wait_ge(s("ld_cache_kr_t"), 16)
                        for h in range(HEADS):
                            nc.scalar.activation(k_h[NOPE:QK, h, 0:N], kr_new, ACT.Copy).then_inc(s("kh_rope"), 1)
                            nc.scalar.activation(k_h[NOPE:QK, h, N:NALL], kr_past[:], ACT.Copy).then_inc(s("kh_rope"), 1)
                        for u, (qt, h) in enumerate(units):
                            b, nk = u % 2, len(keys(qt)) * P
                            act.wait_ge(s("negmax"), u + 1)
                            if u >= 2:
                                act.wait_ge(s("turned"), u - 1)
                            src = ps_s[b][:, 0, 0:P] if qt == 0 else ps_s[b][:, :, 0:NH2]
                            dst = probs[b][:, 0:nk] if qt == 0 else halves(probs[b])
                            nc.scalar.activation(dst, src, ACT.Exp, bias=stat[b][:, 1:2], scale=ATT_SCALE,
                                                 accum_out=stat[b][:, 2:3]).then_inc(s("exp"), 1)

                    @block.vector
                    def _(dve):
                        link = Chain(dve, s("dve2"))
                        dve.wait_ge(s("cq_meansq"), 1)
                        rstd_ops(dve, link, "cq", ps_s[0][:, :, 0:NH2], halves(var), var, root, r, t)
                        for k in (0, 1):
                            ins = nc.vector.scalar_tensor_tensor(
                                out=proj[:, M_CQ + k, :], in0=proj[:, M_CQ + k, :],
                                scalar=cols[:, C_QN + k:C_QN + k + 1], in1=r, op0=ALU.mult, op1=ALU.mult)
                            ins.then_inc(s("cq_normed"), 1)
                        dve.wait_ge(s("cq_normed"), 2)
                        dve.wait_ge(s("ckv_meansq"), 1)
                        rstd_ops(dve, link, "ckv", ps_s[1][:, :, 0:NH2], halves(var), var, root, r, t)
                        nc.vector.scalar_tensor_tensor(
                            out=ckv[:, 0:N], in0=proj[:, M_CKV, :], scalar=cols[:, C_KVN:C_KVN + 1],
                            in1=r, op0=ALU.mult, op1=ALU.mult).then_inc(s("ckv_normed"), 1)
                        dve.wait_ge(s("ld_cos_t"), 16)
                        dve.wait_ge(s("ld_sin_t"), 16)
                        link(nc.vector.tensor_copy(kr_new[:, 0:NCTX], proj[0:ROPE, M_KR, 0:NCTX]))
                        link(nc.vector.tensor_tensor(t1[0:ROPE], proj[0:ROPE, M_KR, NCTX:N], cos_t[0:ROPE, :], ALU.mult))
                        link(nc.vector.tensor_tensor(t2[0:ROPE], proj[ROPE:2 * ROPE, M_KR, NCTX:N],
                                                     sin_t[ROPE:2 * ROPE, :], ALU.mult))
                        nc.vector.tensor_tensor(kr_new[:, NCTX:N], t1[0:ROPE], t2[0:ROPE], ALU.add
                                                ).then_inc(s("kr_done"), 1)
                        dve.wait_ge(s("ctx_turned"), 1)
                        nc.vector.tensor_copy(ckv_out[:, 0:P], ps_t[:, 0, 0:P]).then_inc(s("ckv_out"), 1)
                        nc.vector.tensor_copy(ckv_out[:, P:P + ROPE], ps_t[:, 1, 0:ROPE]).then_inc(s("ckv_out"), 1)
                        for m in range(4):
                            b = m % 2
                            dve.wait_ge(s("q_nope"), m + 1)
                            for j in (0, 1):
                                ins = nc.vector.tensor_copy(halves(q_h[0:NOPE, 2 * m + j, :]),
                                                            ps_s[b][NOPE * j:NOPE * j + NOPE, :, 0:NH2])
                            ins.then_inc(s("q_nope_read"), 1)
                        for m in (0, 1):
                            dve.wait_ge(s("q_rope"), m + 1)
                            for j in range(4):
                                rows = slice(ROPE * j, ROPE * j + ROPE)
                                link(nc.vector.tensor_copy(q_h[NOPE:QK, 4 * m + j, 0:NCTX], ps_s[0][rows, 0, 0:NCTX]))
                            pieces = ((0, NCTX, NH2), (1, 0, NH2))
                            at = 0
                            for bank, c0, c1_ in pieces:
                                w = c1_ - c0
                                link(nc.vector.tensor_tensor(t1[:, at:at + w], ps_s[0][:, bank, c0:c1_],
                                                             cos_t[:, at:at + w], ALU.mult))
                                link(nc.vector.tensor_tensor(t2[:, at:at + w], ps_s[1][:, bank, c0:c1_],
                                                             sin_t[:, at:at + w], ALU.mult))
                                at += w
                            for j in range(4):
                                rows = slice(ROPE * j, ROPE * j + ROPE)
                                ins = nc.vector.tensor_tensor(q_h[NOPE:QK, 4 * m + j, NCTX:N], t1[rows], t2[rows], ALU.add)
                                ins.then_inc(s("q_rope_read"), 1)
                        for m in range(4):
                            b = m % 2
                            dve.wait_ge(s("k_nope"), m + 1)
                            for j in (0, 1):
                                ins = nc.vector.tensor_copy(
                                    k_h[0:NOPE, 2 * m + j, :].rearrange("p (h n) -> p h n", h=2),
                                    ps_s[b][NOPE * j:NOPE * j + NOPE, :, 0:NALL // 2])
                            ins.then_inc(s("k_nope_read"), 1)
                        for kt in range(NALL // P):
                            dve.wait_ge(s("v_ps"), kt + 1)
                            nc.vector.tensor_copy(v_tok[:, kt, :], ps_o[kt % 2][:, :]).then_inc(s("v_read"), 1)

                        def maximum(u):
                            qt, h = units[u]
                            b = u % 2
                            dve.wait_ge(s("scores"), u + 1)
                            src = ps_s[b][:, 0, 0:P] if qt == 0 else ps_s[b][:, :, 0:NH2]
                            link(nc.vector.tensor_reduce(stat[b][:, 0:1], src, AX.X if qt == 0 else AX.XY, ALU.max))
                            nc.vector.tensor_scalar(stat[b][:, 1:2], stat[b][:, 0:1], -ATT_SCALE, None,
                                                    ALU.mult).then_inc(s("negmax"), 1)

                        def normalise(u):
                            qt, h = units[u]
                            b, nk = u % 2, len(keys(qt)) * P
                            dve.wait_ge(s("exp"), u + 1)
                            link(nc.vector.reciprocal(stat[b][:, 3:4], stat[b][:, 2:3]))
                            nc.vector.tensor_scalar(probs[b][:, 0:nk], probs[b][:, 0:nk], stat[b][:, 3:4], None,
                                                    ALU.mult).then_inc(s("probs"), 1)

                        def read_turned(u):
                            qt, h = units[u]
                            b, n = u % 2, len(keys(qt))
                            dve.wait_ge(s("turned"), u + 1)
                            if u >= 2:
                                dve.wait_ge(s("attended"), u - 1)
                            if n == 1:
                                nc.vector.tensor_copy(probs_t[b][:, 0:P], ps_t[:, 0, 0:P]).then_inc(s("probs_t"), 1)
                            else:
                                nc.vector.tensor_copy(probs_t[b][:, 0:384], ps_t[:, 0, 0:384]).then_inc(s("probs_ta"), 1)
                                nc.vector.tensor_copy(probs_t[b][:, 384:N], ps_t[:, 1, 0:256]).then_inc(s("probs_t"), 1)

                        def read_out(u):
                            qt, h = units[u]
                            b = u % 2
                            dve.wait_ge(s("attended"), u + 1)
                            rows = slice(VD * (h % 2), VD * (h % 2) + VD)
                            cs = slice(qt * P, qt * P + P)
                            nc.vector.tensor_copy(h_hi[rows, h // 2, cs], ps_o[b][rows, 0:P]).then_inc(s("att_hi"), 1)
                            dve.wait_ge(s("att_hi"), u + 1)
                            nc.vector.tensor_tensor(h_lo[rows, h // 2, cs], ps_o[b][rows, 0:P],
                                                    h_hi[rows, h // 2, cs].bitcast(F32), ALU.subtract
                                                    ).then_inc(s("att_read"), 1)
                        for u in range(len(units) + 2):
                            if u < len(units):
                                maximum(u)
                            if 1 <= u <= len(units):
                                normalise(u - 1)
                                read_turned(u - 1)
                            if u >= 2:
                                read_out(u - 2)

                    @block.tensor
                    def _(pe):
                        for name in ("inv_q", "inv_k", "w_uq", "w_ukv", "cache_ckv_t"):
                            pe.wait_ge(s("ld_" + name), 16)
                        pe.wait_ge(s("lat_sq"), 2)
                        for half in (0, 1):
                            cs = slice(half * NH2, half * NH2 + NH2)
                            nc.tensor.matmul(ps_s[0][:, half, 0:NH2], inv_q[:], sq[:, cs], start=True, stop=False)
                            last = nc.tensor.matmul(ps_s[0][:, half, 0:NH2], inv_q[:], sqb[:, cs], start=False, stop=True)
                        last.then_inc(s("cq_meansq"), 1)
                        pe.wait_ge(s("lat_sq"), 3)
                        for half in (0, 1):
                            cs = slice(half * NH2, half * NH2 + NH2)
                            last = nc.tensor.matmul(ps_s[1][:, half, 0:NH2], inv_k[:], sq[:, cs], start=True, stop=True)
                        last.then_inc(s("ckv_meansq"), 1)
                        pe.wait_ge(s("ckv_normed"), 1)
                        nc.tensor.transpose(ps_t[:, 0, 0:P], ckv[:, 0:NCTX], ident[:])
                        pe.wait_ge(s("kr_done"), 1)
                        nc.tensor.transpose(ps_t[:, 1, 0:ROPE], kr_new[:, 0:NCTX], ident[0:ROPE, 0:ROPE]
                                            ).then_inc(s("ctx_turned"), 1)

                        def q_product(ps, c0):
                            for half in (0, 1):
                                for k in (0, 1):
                                    ins = nc.tensor.matmul(ps[:, half, 0:NH2], w_uq[:, k, c0:c0 + P],
                                                           proj[:, M_CQ + k, half * NH2:half * NH2 + NH2],
                                                           start=(k == 0), stop=(k == 1))
                            return ins
                        pe.wait_ge(s("cq_normed"), 2)
                        for m in range(4):
                            if m >= 2:
                                pe.wait_ge(s("q_nope_read"), m - 1)
                            q_product(ps_s[m % 2], m * P).then_inc(s("q_nope"), 1)
                        pe.wait_ge(s("q_nope_read"), 4)
                        for m in (0, 1):
                            if m:
                                pe.wait_ge(s("q_rope_read"), 4 * m)
                            q_product(ps_s[0], 512 + m * P)
                            q_product(ps_s[1], 768 + m * P).then_inc(s("q_rope"), 1)
                        pe.wait_ge(s("q_rope_read"), 8)
                        for m in range(4):
                            if m >= 2:
                                pe.wait_ge(s("k_nope_read"), m - 1)
                            for half in (0, 1):
                                last = nc.tensor.matmul(ps_s[m % 2][:, half, 0:NALL // 2], w_ukv[:, 0, m * P:m * P + P],
                                                        ckv[:, half * (NALL // 2):(half + 1) * (NALL // 2)],
                                                        start=True, stop=True)
                            last.then_inc(s("k_nope"), 1)
                        for kt in range(NALL // P):
                            if kt >= 2:
                                pe.wait_ge(s("v_read"), kt - 1)
                            nc.tensor.matmul(ps_o[kt % 2][:, :], ckv[:, kt * P:kt * P + P], w_ukv[:, 1, :],
                                             start=True, stop=True).then_inc(s("v_ps"), 1)
                        pe.wait_ge(s("k_nope_read"), 4)
                        pe.wait_ge(s("v_read"), NALL // P)
                        pe.wait_ge(s("kh_rope"), 2 * HEADS)

                        def score(u):
                            qt, h = units[u]
                            if u >= 2:
                                pe.wait_ge(s("exp"), u - 1)
                            q = q_h[:, h, qt * P:qt * P + P]
                            if qt == 0:
                                last = nc.tensor.matmul(ps_s[u % 2][:, 0, 0:P], q, k_h[:, h, 0:P], start=True, stop=True)
                            else:
                                for half in (0, 1):
                                    c0 = P + half * NH2
                                    last = nc.tensor.matmul(ps_s[u % 2][:, half, 0:NH2], q, k_h[:, h, c0:c0 + NH2],
                                                            start=True, stop=True)
                            last.then_inc(s("scores"), 1)

                        def turn(u):
                            qt, h = units[u]
                            pe.wait_ge(s("probs"), u + 1)
                            if u:
                                pe.wait_ge(s("probs_t"), u)
                            for j in range(len(keys(qt))):
                                out = ps_t[:, j // 3, (j % 3) * P:(j % 3) * P + P]
                                last = nc.tensor.transpose(out, probs[u % 2][:, j * P:j * P + P], ident[:])
                            last.then_inc(s("turned"), 1)

                        def attend(u):
                            qt, h = units[u]
                            pe.wait_ge(s("probs_t"), u + 1)
                            if u >= 2:
                                pe.wait_ge(s("att_read"), u - 1)
                            kts = keys(qt)
                            r0 = VD * (h % 2)
                            for j, kt in enumerate(kts):
                                last = nc.tensor.matmul(ps_o[u % 2][r0:r0 + VD, 0:P], v_tok[:, kt, h * VD:h * VD + VD],
                                                        probs_t[u % 2][:, j * P:j * P + P],
                                                        start=(j == 0), stop=(j == len(kts) - 1))
                            last.then_inc(s("attended"), 1)
                        for u in range(len(units) + 2):
                            if u < len(units):
                                score(u)
                            if 1 <= u <= len(units):
                                turn(u - 1)
                            if u >= 2:
                                attend(u - 2)

                s.clear()

                with ExitStack() as c3:
                    W = NLAT + 384
                    rel = [sb(c3, f"rel{g}", [P, W]) for g in (0, 1)]
                    msk = [sb(c3, f"msk{g}", [P, W]) for g in (0, 1)]
                    dec = [sb(c3, f"dec{g}", [P, W]) for g in (0, 1)]
                    dmat = [sb(c3, f"dmat{h}", [P, W]) for h in range(RH)]
                    steps = sb(c3, "steps", [P, 2, NLAT])
                    ksteps = sb(c3, "ksteps", [P, 2 * RH])
                    state = sb(c3, "state", [P, 2, RH, DK])
                    inv_e = sb(c3, "inv_e", [P, P])
                    rv_tok = sb(c3, "rv_tok", [P, NT, 512])
                    rk_tok = sb(c3, "rk_tok", [P, 512])
                    kdec = sb(c3, "kdec", [P, 2, 512])
                    lgw = sb(c3, "lgw", [P, 8, 8])
                    scm = [sb(c3, f"scm{b}", [P, NLAT]) for b in (0, 1)]
                    qdec = [sb(c3, f"qdec{g}", [P, NLAT]) for g in (0, 1)]
                    st_out = sb(c3, "st_out", [P, 2, RH, DK])
                    y_t = act_buf
                    var, root, r, t = (act_buf[:, k, :] for k in (4, 5, 6, 7))
                    ps_sc = [pb(c3, f"ps_sc{b}", [P, 512]) for b in (0, 1)]
                    ps_y = [pb(c3, f"ps_y{b}", [P, 512]) for b in (0, 1)]
                    ps_n = pb(c3, "ps_n3", [P, 2, 512])
                    units = [(h, j) for h in range(RH) for j in range(NT)]
                    lg = lgw[:, 7, :]
                    block = c3.enter_context(nc.Block())

                    @block.sync
                    def _(sp):
                        for dst, name in ((rel[0][:], "rel0"), (rel[1][:], "rel1"), (msk[0][:], "msk0"),
                                          (msk[1][:], "msk1"), (steps[:], "steps"), (ksteps[:], "ksteps"),
                                          (state[:], "state"), (inv_e[:], "inv_k")):
                            sp.dma_start(dst, a[name]).then_inc(s("ret_ld"), 16)
                        sp.wait_ge(s("st_read"), 2 * RH)
                        for g, dst in ((0, new_sf), (1, new_sb)):
                            sp.dma_start(dst, st_out[:, g, :, :]).then_inc(s("st_state"), 16)
                        sp.wait_ge(s("st_state"), 32)

                    @block.scalar
                    def _(act):
                        act.wait_ge(s("lg_abs"), 1)
                        nc.scalar.activation(lgw[:, 1, :], lgw[:, 0, :], ACT.Exp, scale=-1.0).then_inc(s("lg_exp"), 1)
                        act.wait_ge(s("lg_done"), 1)
                        act.wait_ge(s("ret_ld"), 16 * 8)
                        act.wait_ge(s("kst_mul"), 1)
                        nc.scalar.activation(ksteps[:], ksteps[:], ACT.Exp).then_inc(s("kst_exp"), 1)
                        for h in range(RH):
                            for g in (0, 1):
                                if h:
                                    act.wait_ge(s("dmat"), h)
                                nc.scalar.activation(dec[g][:], rel[g][:], ACT.Exp, scale=lg[:, RH * g + h:RH * g + h + 1]
                                                     ).then_inc(s("dec"), 1)
                        for h in range(RH):
                            for g in (0, 1):
                                if h:
                                    act.wait_ge(s("ret_av"), NT * h)
                                nc.scalar.activation(qdec[g][:], steps[:, g, :], ACT.Exp,
                                                     scale=lg[:, RH * g + h:RH * g + h + 1]).then_inc(s("qexp"), 1)
                        for h in range(RH):
                            act.wait_ge(s("centred"), h + 1)
                            if h:
                                act.wait_ge(s("gn_normed"), h)
                            nc.scalar.activation(t, y_t[:, h, :], ACT.Square).then_inc(s("gn_sq"), 1)
                            act.wait_ge(s(f"gn{h}_var"), 1)
                            nc.scalar.activation(root, var, ACT.Sqrt).then_inc(s(f"gn{h}_root"), 1)
                            nc.scalar.activation(proj[:, M_RG + h, :], proj[:, M_RG + h, :], ACT.Silu).then_inc(s("silu_g"), 1)
                            act.wait_ge(s("ret_out"), h + 1)
                            nc.scalar.activation(h_hi[:, RH + h, :], y_t[:, h, :], ACT.Copy).then_inc(s("ret_hi"), 1)

                    @block.vector
                    def _(dve):
                        link = Chain(dve, s("dve3"))
                        V = nc.vector
                        x = cols[:, C_LOG:C_LOG + 8]
                        link(V.tensor_scalar(lgw[:, 0, :], x, -1.0, None, ALU.mult))
                        V.tensor_tensor(lgw[:, 0, :], lgw[:, 0, :], x, ALU.max).then_inc(s("lg_abs"), 1)
                        dve.wait_ge(s("lg_exp"), 1)
                        link(V.tensor_scalar(lgw[:, 2, :], lgw[:, 1, :], 2.0, None, ALU.add))
                        link(V.reciprocal(lgw[:, 3, :], lgw[:, 2, :]))
                        link(V.tensor_tensor(lgw[:, 4, :], lgw[:, 1, :], lgw[:, 3, :], ALU.mult))
                        link(V.tensor_tensor(lgw[:, 5, :], lgw[:, 4, :], lgw[:, 4, :], ALU.mult))
                        link(V.tensor_scalar(lgw[:, 6, :], lgw[:, 5, :], 1 / 19, 1 / 17, ALU.mult, ALU.add))
                        for n in range(15, 0, -2):
                            link(V.tensor_tensor(lgw[:, 6, :], lgw[:, 6, :], lgw[:, 5, :], ALU.mult))
                            link(V.tensor_scalar(lgw[:, 6, :], lgw[:, 6, :], 1 / n, None, ALU.add))
                        link(V.tensor_tensor(lgw[:, 6, :], lgw[:, 6, :], lgw[:, 4, :], ALU.mult))
                        link(V.tensor_scalar(lgw[:, 0, :], x, 0.0, None, ALU.min))
                        V.scalar_tensor_tensor(out=lg, in0=lgw[:, 6, :], scalar=-2.0, in1=lgw[:, 0, :],
                                               op0=ALU.mult, op1=ALU.add).then_inc(s("lg_done"), 1)
                        dve.wait_ge(s("lg_done"), 1)
                        dve.wait_ge(s("ret_ld"), 16 * 8)
                        V.tensor_tensor(ksteps[:], ksteps[:], lg, ALU.mult).then_inc(s("kst_mul"), 1)
                        for k in range(NT + 1):
                            dve.wait_ge(s("turned3"), k + 1)
                            dst = rv_tok[:, k, :] if k < NT else rk_tok[:, :]
                            V.tensor_copy(dst, ps_sc[k % 2][:, :]).then_inc(s("turned3_read"), 1)
                        dve.wait_ge(s("turned3_read"), NT + 1)
                        dve.wait_ge(s("kst_exp"), 1)
                        for g in (0, 1):
                            for h in range(RH):
                                cs = slice(h * DK, h * DK + DK)
                                V.tensor_scalar(kdec[:, g, cs], rk_tok[:, cs], ksteps[:, RH * g + h:RH * g + h + 1],
                                                RET_SCALE, ALU.mult, ALU.mult).then_inc(s("kdec"), 1)
                        for g in (0, 1):
                            for h in range(RH):
                                k = g * RH + h
                                dve.wait_ge(s("st_mm"), k + 1)
                                V.tensor_copy(st_out[:, g, h, :], ps_y[k % 2][:, 0:DK]).then_inc(s("st_read"), 1)
                        for h in range(RH):
                            dve.wait_ge(s("dec"), 2 * h + 2)
                            link(V.tensor_tensor(dec[0][:], dec[0][:], msk[0][:], ALU.mult))
                            link(V.tensor_tensor(dec[1][:], dec[1][:], msk[1][:], ALU.mult))
                            V.tensor_tensor(dmat[h][:], dec[0][:], dec[1][:], ALU.add).then_inc(s("dmat"), 1)
                        dve.wait_ge(s("dmat"), RH)
                        for u, (h, j) in enumerate(units):
                            if j == 0:
                                dve.wait_ge(s("qexp"), 2 * h + 2)
                                for g in (0, 1):
                                    V.tensor_tensor(qdec[g][:], qdec[g][:], proj[:, M_RQ + h, NCTX:N], ALU.mult
                                                    ).then_inc(s("qdec"), 1)
                            dve.wait_ge(s("ret_sc"), u + 1)
                            if u >= 2:
                                dve.wait_ge(s("ret_av"), u - 1)
                            n, c0 = (NCTX, 384) if j == 0 else (NLAT, 384 - P * (j - 1))
                            V.scalar_tensor_tensor(out=scm[u % 2][:, 0:n], in0=ps_sc[u % 2][:, 0:n], scalar=RET_SCALE,
                                                   in1=dmat[h][:, c0:c0 + n], op0=ALU.mult, op1=ALU.mult
                                                   ).then_inc(s("ret_masked"), 1)
                            if j == 1:
                                dve.wait_ge(s("ret_av"), 5 * h + 1)
                                V.tensor_copy(y_t[:, h, 0:NCTX], ps_y[0][:, 0:NCTX]).then_inc(s("y_ctx"), 1)
                            if j == NT - 1:
                                dve.wait_ge(s("ret_av"), NT * h + NT)
                                V.tensor_copy(y_t[:, h, NCTX:N], ps_y[1][:, :]).then_inc(s("y_lat"), 1)
                        dve.wait_ge(s("y_lat"), RH)
                        for h in range(RH):
                            dve.wait_ge(s("gn_mean"), h + 1)
                            V.tensor_tensor(halves(y_t[:, h, :]), halves(y_t[:, h, :]), ps_n[:, :, 0:NH2], ALU.subtract
                                            ).then_inc(s("centred"), 1)
                            dve.wait_ge(s("gn_var"), h + 1)
                            rstd_ops(dve, link, f"gn{h}", ps_n[:, :, 0:NH2], halves(var), var, root, r, t)
                            V.scalar_tensor_tensor(out=y_t[:, h, :], in0=y_t[:, h, :], scalar=cols[:, C_GN + h:C_GN + h + 1],
                                                   in1=r, op0=ALU.mult, op1=ALU.mult).then_inc(s("gn_normed"), 1)
                            dve.wait_ge(s("gn_normed"), h + 1)
                            dve.wait_ge(s("silu_g"), h + 1)
                            V.tensor_tensor(y_t[:, h, :], y_t[:, h, :], proj[:, M_RG + h, :], ALU.mult
                                            ).then_inc(s("ret_out"), 1)
                            dve.wait_ge(s("ret_hi"), h + 1)
                            V.tensor_tensor(h_lo[:, RH + h, :], y_t[:, h, :], h_hi[:, RH + h, :].bitcast(F32), ALU.subtract
                                            ).then_inc(s("ret_lo"), 1)

                    @block.tensor
                    def _(pe):
                        pe.wait_ge(s("ret_ld"), 16 * 8)
                        for k in range(NT + 1):
                            if k >= 2:
                                pe.wait_ge(s("turned3_read"), k - 1)
                            for h in range(RH):
                                src = proj[:, M_RV + h, k * P:k * P + P] if k < NT else proj[:, M_RK + h, 0:P]
                                last = nc.tensor.transpose(ps_sc[k % 2][:, h * P:h * P + P], src, ident[:])
                            last.then_inc(s("turned3"), 1)
                        pe.wait_ge(s("turned3_read"), NT + 1)
                        pe.wait_ge(s("kdec"), 2 * RH)
                        for k in range(2 * RH):
                            g, h = k // RH, k % RH
                            cs = slice(h * DK, h * DK + DK)
                            if k >= 2:
                                pe.wait_ge(s("st_read"), k - 1)
                            nc.tensor.matmul(ps_y[k % 2][:, 0:DK], kdec[:, g, cs], rv_tok[:, 0, cs], start=True, stop=True
                                             ).then_inc(s("st_mm"), 1)
                        pe.wait_ge(s("st_read"), 2 * RH)

                        def score(u):
                            h, j = units[u]
                            if u >= 2:
                                pe.wait_ge(s("ret_masked"), u - 1)
                            qs = slice(0, NCTX) if j == 0 else slice(NCTX, N)
                            nc.tensor.matmul(ps_sc[u % 2][:, 0:qs.stop - qs.start], proj[:, M_RK + h, j * P:j * P + P],
                                             proj[:, M_RQ + h, qs], start=True, stop=True).then_inc(s("ret_sc"), 1)

                        def values(u):
                            h, j = units[u]
                            pe.wait_ge(s("ret_masked"), u + 1)
                            v = rv_tok[:, j, h * DK:h * DK + DK]
                            if j == 0:
                                if h:
                                    pe.wait_ge(s("y_ctx"), h)
                                nc.tensor.matmul(ps_y[0][:, 0:NCTX], v, scm[u % 2][:, 0:NCTX], start=True, stop=True
                                                 ).then_inc(s("ret_av"), 1)
                                return
                            if j == 1:
                                if h:
                                    pe.wait_ge(s("y_lat"), h)
                                pe.wait_ge(s("qdec"), 2 * h + 2)
                                for g in (0, 1):
                                    nc.tensor.matmul(ps_y[1][:, :], state[:, g, h, :], qdec[g][:], start=(g == 0), stop=False)
                            last = nc.tensor.matmul(ps_y[1][:, :], v, scm[u % 2][:, :], start=False, stop=(j == NT - 1))
                            last.then_inc(s("ret_av"), 1)
                        for u in range(len(units) + 1):
                            if u < len(units):
                                score(u)
                            if u:
                                values(u - 1)
                        pe.wait_ge(s("y_lat"), RH)
                        pe.wait_ge(s("y_ctx"), RH)
                        for h in range(RH):
                            if h:
                                pe.wait_ge(s(f"gn{h - 1}_var"), 1)
                            for half in (0, 1):
                                last = nc.tensor.matmul(ps_n[:, half, 0:NH2], inv_e[:], y_t[:, h, half * NH2:half * NH2 + NH2],
                                                        start=True, stop=True)
                            last.then_inc(s("gn_mean"), 1)
                            pe.wait_ge(s("gn_sq"), h + 1)
                            for half in (0, 1):
                                last = nc.tensor.matmul(ps_n[:, half, 0:NH2], inv_e[:], t[:, half * NH2:half * NH2 + NH2],
                                                        start=True, stop=True)
                            last.then_inc(s("gn_var"), 1)

            s.clear()

            with ExitStack() as c4:
                banks = [pb(c4, f"mrg_ps{b}", [P, 4, 512]) for b in (0, 1)]
                with ExitStack() as c:
                    gbuf = [[sb(c, f"gbuf{g}{b}", [P, N]) for b in (0, 1)] for g in (0, 1)]
                    prt = [sb(c, f"prt{b}", [P, N]) for b in (0, 1)]
                    lin = Linear(c, "mrg", a["w_up"], KC, banks)
                    block = c.enter_context(nc.Block())

                    @block.sync
                    def _(sp):
                        def step(i):
                            for b in (0, 1):
                                lin.load(sp, i, b)
                                sp.wait_ge(lin.sem("evac", b), i)
                                for g in (0, 1):
                                    sp.dma_start(gbuf[g][b][:], gates_d[bass.ds(2 * i + b + KC * g, 1)].rearrange("o p m -> p (o m)")
                                                 ).then_inc(s(f"gate_ld{b}{g}"), 16)
                        run(sp, 0, KC // 2, step)

                    @block.scalar
                    def _(act):
                        def step(i):
                            for b in (0, 1):
                                lin.head(act, i, b)
                        run(act, 0, KC // 2, step)

                    @block.gpsimd
                    def _(pool):
                        def step(i):
                            for b in (0, 1):
                                lin.rest(pool, i, b)
                        run(pool, 0, KC // 2, step)

                    @block.vector
                    def _(dve):
                        def step(i):
                            for b in (0, 1):
                                lin.wait_out(dve, i, b)
                                for g in (0, 1):
                                    dve.wait_ge(s(f"gate_ld{b}{g}"), 16 * i + 16)
                                nc.vector.tensor_tensor(halves(prt[b][:, :]), lin.out(b, 0), halves(gbuf[0][b][:, :]), ALU.mult
                                                        ).then_inc(s(f"prt_a{b}"), 1)
                                nc.vector.tensor_tensor(halves(gbuf[1][b][:, :]), lin.out(b, 1), halves(gbuf[1][b][:, :]), ALU.mult
                                                        ).then_inc(s(f"prt_b{b}"), 1)
                                dve.wait_ge(s(f"prt_a{b}"), i + 1)
                                dve.wait_ge(s(f"prt_b{b}"), i + 1)
                                nc.vector.tensor_tensor(act_buf[:, bass.ds(2 * i + b, 1), :].rearrange("p o n -> p (o n)"),
                                                        prt[b][:, :], gbuf[1][b][:, :], ALU.add).then_inc(lin.sem("evac", b), 1)
                        run(dve, 0, KC // 2, step)

                    @block.tensor
                    def _(pe):
                        def step(i):
                            for b in (0, 1):
                                lin.product(pe, i, b, ((0, 4), (4, 8)))
                        run(pe, 0, KC // 2, step)

                def split_act(act, tag):
                    for kc in range(KC):
                        nc.scalar.activation(h_hi[:, kc, :], act_buf[:, kc, :], ACT.Copy).then_inc(s(tag + "_hi"), 1)

                def split_dve(dve, tag):
                    for kc in range(KC):
                        dve.wait_ge(s(tag + "_hi"), kc + 1)
                        nc.vector.tensor_tensor(h_lo[:, kc, :], act_buf[:, kc, :], h_hi[:, kc, :].bitcast(F32),
                                                ALU.subtract).then_inc(s(tag + "_split"), 1)

                with ExitStack() as c:
                    lin = Linear(c, "wo", a["w_o"], KC, banks)
                    inv_d = sb(c, "inv_d4", [P, P])
                    wrk = [sb(c, f"n2_{n}", [P, N]) for n in ("var", "root", "r", "t")]
                    x2_tok = [sb(c, f"x2_tok{b}", [P, D]) for b in (0, 1)]
                    block = c.enter_context(nc.Block())

                    @block.sync
                    def _(sp):
                        sp.dma_start(inv_d[:], a["inv_d"]).then_inc(s("ld_inv4"), 16)
                        def step(i):
                            for b in (0, 1):
                                lin.load(sp, i, b)
                        run(sp, 0, KC // 2, step)
                        for tt in range(NT):
                            sp.wait_ge(s("x2_read"), 2 * tt + 2)
                            sp.dma_start(x2_d[tt], x2_tok[tt % 2][:]).then_inc(s(f"x2_st{tt % 2}"), 16)
                        sp.wait_ge(s("x2_st0"), 48)
                        sp.wait_ge(s("x2_st1"), 32)

                    @block.scalar
                    def _(act):
                        split_act(act, "m")
                        def step(i):
                            for b in (0, 1):
                                lin.head(act, i, b)
                        run(act, 0, KC // 2, step)
                        for b in (0, 1):
                            act.wait_ge(lin.sem("evac", b), KC // 2)
                        for kc in range(KC):
                            nc.scalar.activation(act_buf[:, kc, :], x_t[:, kc, :], ACT.Square).then_inc(s("n2_sq"), 1)
                        norm_act(act, "n2", wrk)

                    @block.gpsimd
                    def _(pool):
                        def step(i):
                            for b in (0, 1):
                                lin.rest(pool, i, b)
                        run(pool, 0, KC // 2, step)

                    @block.vector
                    def _(dve):
                        link = Chain(dve, s("dve4"))
                        split_dve(dve, "m")
                        def step(i):
                            for b in (0, 1):
                                lin.wait_out(dve, i, b)
                                m = 2 * i + b
                                xm = x_t[:, bass.ds(m, 1), :].rearrange("p o n -> p (o n)")
                                gm = [mod[:, bass.ds(m + 2 * KC, 1), g] for g in (0, 1)]
                                ps = lin.ps[b]
                                for g, bank, c0, c1_, x0 in ((0, 0, 0, NCTX, 0), (1, 0, NCTX, NH2, NCTX), (1, 1, 0, NH2, NH2)):
                                    ins = nc.vector.scalar_tensor_tensor(
                                        out=xm[:, x0:x0 + c1_ - c0], in0=ps[:, bank, c0:c1_], scalar=gm[g],
                                        in1=xm[:, x0:x0 + c1_ - c0], op0=ALU.mult, op1=ALU.add)
                                ins.then_inc(lin.sem("evac", b), 1)
                        run(dve, 0, KC // 2, step)
                        norm_dve(dve, link, "n2", banks[0][:, 0:2, :], wrk, C_FFN, 3 * KC, 4 * KC)
                        for k in range(2 * NT):
                            if k >= 4:
                                dve.wait_ge(s(f"x2_st{(k // 2) % 2}"), 16 * (k // 4))
                            dve.wait_ge(s("x2_turned"), k + 1)
                            nc.vector.tensor_copy(x2_tok[(k // 2) % 2][:, 512 * (k % 2):512 * (k % 2) + 512],
                                                  banks[1][:, k % 4, :]).then_inc(s("x2_read"), 1)

                    @block.tensor
                    def _(pe):
                        pe.wait_ge(s("m_split"), KC)
                        def step(i):
                            for b in (0, 1):
                                lin.product(pe, i, b)
                        run(pe, 0, KC // 2, step)
                        for b in (0, 1):
                            pe.wait_ge(lin.sem("evac", b), KC // 2)
                        pe.wait_ge(s("ld_inv4"), 16)
                        norm_pe(pe, "n2", act_buf, inv_d, banks[0], "n2_sq")
                        for k in range(2 * NT):
                            if k >= 4:
                                pe.wait_ge(s("x2_read"), k - 3)
                            for j in range(4):
                                last = nc.tensor.transpose(banks[1][:, k % 4, j * P:j * P + P],
                                                           x_t[:, 4 * (k % 2) + j, (k // 2) * P:(k // 2) * P + P], ident[:])
                            last.then_inc(s("x2_turned"), 1)

                with ExitStack() as c:
                    lin = Linear(c, "wq", a["w_q"], 16, banks)
                    q_t = sb(c, "q_t", [P, 16, N])
                    keys_t = sb(c, "keys_t", [P, 16, NK])
                    sc_tok = [sb(c, f"sc_tok{b}", [P, 16 * NK]) for b in (0, 1)]
                    block = c.enter_context(nc.Block())

                    @block.sync
                    def _(sp):
                        sp.dma_start(keys_t[:], a["keys_t"]).then_inc(s("ld_keys"), 16)
                        def step(i):
                            for b in (0, 1):
                                lin.load(sp, i, b)
                        run(sp, 0, 8, step)
                        for tt in range(NT):
                            sp.wait_ge(s("sc_read"), 4 * tt + 4)
                            sp.dma_start(scores_d[tt], sc_tok[tt % 2][:]).then_inc(s(f"sc_st{tt % 2}"), 16)
                        sp.wait_ge(s("sc_st0"), 48)
                        sp.wait_ge(s("sc_st1"), 32)

                    @block.scalar
                    def _(act):
                        def step(i):
                            for b in (0, 1):
                                lin.head(act, i, b)
                        run(act, 0, 8, step)

                    @block.gpsimd
                    def _(pool):
                        def step(i):
                            for b in (0, 1):
                                lin.rest(pool, i, b)
                        run(pool, 0, 8, step)

                    @block.vector
                    def _(dve):
                        def step(i):
                            for b in (0, 1):
                                lin.wait_out(dve, i, b)
                                nc.vector.tensor_copy(
                                    q_t[:, bass.ds(2 * i + b, 1), :].rearrange("p o (h n) -> p (o h) n", h=2),
                                    lin.out(b)).then_inc(lin.sem("evac", b), 1)
                        run(dve, 0, 8, step)
                        for k in range(4 * NT):
                            if k >= 8:
                                dve.wait_ge(s(f"sc_st{(k // 4) % 2}"), 16 * (k // 8))
                            dve.wait_ge(s("sc_mm"), k + 1)
                            nc.vector.tensor_copy(sc_tok[(k // 4) % 2][:, 512 * (k % 4):512 * (k % 4) + 512],
                                                  banks[0][:, k % 4, :]).then_inc(s("sc_read"), 1)

                    @block.tensor
                    def _(pe):
                        def step(i):
                            for b in (0, 1):
                                lin.product(pe, i, b)
                        run(pe, 0, 8, step)
                        for b in (0, 1):
                            pe.wait_ge(lin.sem("evac", b), 8)
                        pe.wait_ge(s("ld_keys"), 16)
                        for k in range(4 * NT):
                            if k >= 4:
                                pe.wait_ge(s("sc_read"), k - 3)
                            for j in range(4):
                                m = 4 * (k % 4) + j
                                last = nc.tensor.matmul(banks[0][:, k % 4, j * NK:j * NK + NK],
                                                        q_t[:, m, (k // 4) * P:(k // 4) * P + P], keys_t[:, m, :],
                                                        start=True, stop=True)
                            last.then_inc(s("sc_mm"), 1)

        s.clear()

        with ExitStack() as c5:
            sc = sb(c5, "sc", [P, 16, NK])
            sc2 = sb(c5, "sc2", [P, 16, NK])
            val = sb(c5, "val", [P, 16, TOPK])
            idx = sb(c5, "idx", [P, 16, TOPK], U32)
            idxf = sb(c5, "idxf", [P, 16, TOPK])
            cand = sb(c5, "cand", [P, PH, TOPK * TOPK])
            cand2 = sb(c5, "cand2", [P, PH, TOPK * TOPK])
            cval = sb(c5, "cval", [P, PH, TOPK])
            cidx = sb(c5, "cidx", [P, PH, TOPK], U32)
            part = sb(c5, "part", [P, 2, PICKS], U32)
            partf = sb(c5, "partf", [P, 2, PICKS])
            eq = sb(c5, "eq", [P, PICKS, TOPK])
            pick = sb(c5, "pick", [P, 3, PICKS])
            red = sb(c5, "red", [P, 2, PH])
            hold = sb(c5, "hold", [P, 1])
            pick_t = sb(c5, "pick_t", [P, 3, P])
            iota_r = sb(c5, "iota_r", [P, NK])
            o1 = [sb(c5, f"o1_{b}", [P, OB, NK]) for b in (0, 1)]
            o2 = [sb(c5, f"o2_{b}", [P, OB, NK]) for b in (0, 1)]
            stage = [sb(c5, f"stage{b}", [P, NK, WB]) for b in (0, 1)]
            ps_p = pb(c5, "ps_p", [P, 3, P])
            ps_w = [pb(c5, f"ps_w{b}", [P, OB, NK]) for b in (0, 1)]
            NBATCH = P // OB
            block = c5.enter_context(nc.Block())

            @block.sync
            def _(sp):
                sp.dma_start(iota_r[:], a["iota_r"]).then_inc(s("ld_iota"), 16)
                def step(t):
                    sp.wait_ge(s("top1b"), 16 * t)
                    sp.dma_start(sc[:, :, :].rearrange("p m k -> p (m k)"),
                                 scores_d[bass.ds(t, 1)].rearrange("o p m -> p (o m)")).then_inc(s("ld_sc"), 16)
                    for blk in (0, 1):
                        sp.wait_ge(s(f"gates_read{blk}"), (NBATCH // 2) * t + NBATCH // 2)
                        sp.dma_start(wgt_d[:, bass.ds(2 * t + blk, 1), :].rearrange("p o m -> p (o m)"),
                                     stage[blk][:, :, :].rearrange("p k n -> p (k n)")).then_inc(s(f"wgt_st{blk}"), 16)
                run(sp, 0, NT, step)
                for blk in (0, 1):
                    sp.wait_ge(s(f"wgt_st{blk}"), 16 * NT)

            @block.scalar
            def _(act):
                def step(t):
                    act.wait_ge(s("softmax_in"), t + 1)
                    nc.scalar.activation(pick[:, 2, :], pick[:, 2, :], ACT.Exp).then_inc(s("softmax_exp"), 1)
                    for k in range(NBATCH):
                        blk = k // (NBATCH // 2)
                        if k % (NBATCH // 2) == 0:
                            act.wait_ge(s(f"wgt_st{blk}"), 16 * t)
                        act.wait_ge(s(f"gates_mm{k % 2}"), (NBATCH // 2) * t + k // 2 + 1)
                        n0 = (k % (NBATCH // 2)) * OB
                        nc.scalar.activation(stage[blk][:, :, n0:n0 + OB],
                                             ps_w[k % 2][:, :, :].rearrange("p n k -> p k n"), ACT.Copy
                                             ).then_inc(s(f"gates_read{blk}"), 1)
                run(act, 0, NT, step)

            @block.vector
            def _(dve):
                V = nc.vector
                dve.wait_ge(s("ld_iota"), 16)
                def step(t):
                    dve.wait_ge(s("ld_sc"), 16 * t + 16)
                    V.memset(hold[:], 0.0)
                    for m in range(16):
                        V.max(val[:, m, 0:8], sc[:, m, :]).then_inc(s("max1"), 1)
                    dve.wait_ge(s("max1"), 16 * t + 16)
                    V.memset(hold[:], 0.0)
                    for m in range(16):
                        V.max_index(idx[:, m, 0:8], val[:, m, 0:8], sc[:, m, :]).then_inc(s("top1a"), 1)
                    for m in range(16):
                        V.match_replace(sc2[:, m, :], val[:, m, 0:8], sc[:, m, :], LOW).then_inc(s("top1b"), 1)
                    dve.wait_ge(s("top1b"), 16 * t + 16)
                    V.memset(hold[:], 0.0)
                    for m in range(16):
                        V.max(val[:, m, 8:16], sc2[:, m, :]).then_inc(s("max2"), 1)
                    dve.wait_ge(s("max2"), 16 * t + 16)
                    V.memset(hold[:], 0.0)
                    for m in range(16):
                        V.max_index(idx[:, m, 8:16], val[:, m, 8:16], sc2[:, m, :]).then_inc(s("top2"), 1)
                    for h in range(PH):
                        V.tensor_tensor(cand[:, h, :].rearrange("p (a b) -> p a b", a=TOPK),
                                        val[:, 2 * h, :].unsqueeze(2).to_broadcast([P, TOPK, TOPK]),
                                        val[:, 2 * h + 1, :].unsqueeze(1).to_broadcast([P, TOPK, TOPK]),
                                        ALU.add).then_inc(s("cand"), 1)
                    dve.wait_ge(s("cand"), PH * t + PH)
                    V.memset(hold[:], 0.0)
                    for h in range(PH):
                        V.max(cval[:, h, 0:8], cand[:, h, :]).then_inc(s("cmax1"), 1)
                    dve.wait_ge(s("cmax1"), PH * t + PH)
                    V.memset(hold[:], 0.0)
                    for h in range(PH):
                        V.max_index(cidx[:, h, 0:8], cval[:, h, 0:8], cand[:, h, :]).then_inc(s("ctop1a"), 1)
                    for h in range(PH):
                        V.match_replace(cand2[:, h, :], cval[:, h, 0:8], cand[:, h, :], LOW).then_inc(s("ctop1b"), 1)
                    dve.wait_ge(s("ctop1b"), PH * t + PH)
                    V.memset(hold[:], 0.0)
                    for h in range(PH):
                        V.max(cval[:, h, 8:16], cand2[:, h, :]).then_inc(s("cmax2"), 1)
                    dve.wait_ge(s("cmax2"), PH * t + PH)
                    V.memset(hold[:], 0.0)
                    for h in range(PH):
                        V.max_index(cidx[:, h, 8:16], cval[:, h, 8:16], cand2[:, h, :]).then_inc(s("ctop2"), 1)
                    V.tensor_tensor(pick[:, 2, :].rearrange("p (h j) -> p h j", h=PH), cval[:, :, :],
                                    cval[:, :, 0:1].to_broadcast([P, PH, TOPK]), ALU.subtract
                                    ).then_inc(s("softmax_in"), 1)
                    dve.wait_ge(s("ctop2"), PH * t + PH)
                    flat = cidx[:, :, :].rearrange("p h j -> p (h j)")
                    V.tensor_scalar(part[:, 0, :], flat, 4, None, ALU.logical_shift_right).then_inc(s("part"), 1)
                    V.tensor_scalar(part[:, 1, :], flat, 15, None, ALU.bitwise_and).then_inc(s("part"), 1)
                    V.tensor_copy(idxf[:], idx[:]).then_inc(s("part"), 1)
                    dve.wait_ge(s("part"), 3 * t + 3)
                    V.tensor_copy(partf[:], part[:]).then_inc(s("partf"), 1)
                    dve.wait_ge(s("partf"), t + 1)
                    side = idxf[:, :, :].rearrange("p (h s) a -> p s h a", s=2)
                    for g in (0, 1):
                        V.tensor_tensor(eq[:], iota_r[:, 0:TOPK].unsqueeze(1).to_broadcast([P, PICKS, TOPK]),
                                        partf[:, g, :].unsqueeze(2).to_broadcast([P, PICKS, TOPK]),
                                        ALU.is_equal).then_inc(s("eq"), 1)
                        dve.wait_ge(s("eq"), 2 * t + g + 1)
                        V.tensor_tensor(eq[:, :, :].rearrange("p (h j) a -> p h j a", h=PH),
                                        eq[:, :, :].rearrange("p (h j) a -> p h j a", h=PH),
                                        side[:, g].unsqueeze(2).to_broadcast([P, PH, TOPK, TOPK]),
                                        ALU.mult).then_inc(s("eqk"), 1)
                        dve.wait_ge(s("eqk"), 2 * t + g + 1)
                        V.tensor_reduce(pick[:, g, :], eq[:], AX.X, ALU.add).then_inc(s("picked"), 1)
                        dve.wait_ge(s("picked"), 2 * t + g + 1)
                    gates = pick[:, 2, :].rearrange("p (h j) -> p h j", h=PH)
                    dve.wait_ge(s("softmax_exp"), t + 1)
                    V.tensor_reduce(red[:, 0, :], gates, AX.X, ALU.add).then_inc(s("sum"), 1)
                    dve.wait_ge(s("sum"), t + 1)
                    V.reciprocal(red[:, 1, :], red[:, 0, :]).then_inc(s("inv_sum"), 1)
                    dve.wait_ge(s("inv_sum"), t + 1)
                    V.tensor_tensor(gates, gates, red[:, 1, :].unsqueeze(2).to_broadcast([P, PH, TOPK]), ALU.mult
                                    ).then_inc(s("gated"), 1)
                    dve.wait_ge(s("picks_turned"), t + 1)
                    V.tensor_copy(pick_t[:], ps_p[:]).then_inc(s("pick_t"), 1)
                    dve.wait_ge(s("pick_t"), t + 1)
                    iota8 = iota_r[:, :].unsqueeze(1).to_broadcast([P, OB, NK])
                    for k in range(NBATCH):
                        b, cs = k % 2, slice(k * OB, k * OB + OB)

                        def spread(n):
                            return pick_t[:, n, cs].unsqueeze(2).to_broadcast([P, OB, NK])
                        dve.wait_ge(s(f"gates_mm{b}"), (NBATCH // 2) * t + k // 2)
                        V.tensor_tensor(o1[b][:], iota8, spread(0), ALU.is_equal).then_inc(s("oh1"), 1)
                        V.tensor_tensor(o2[b][:], iota8, spread(1), ALU.is_equal).then_inc(s("oh2"), 1)
                        dve.wait_ge(s("oh2"), NBATCH * t + k + 1)
                        V.tensor_tensor(o2[b][:], o2[b][:], spread(2), ALU.mult).then_inc(s("onehot"), 1)
                run(dve, 0, NT, step)

            @block.tensor
            def _(pe):
                def step(t):
                    pe.wait_ge(s("gated"), t + 1)
                    pe.wait_ge(s("picked"), 2 * t + 2)
                    for n in range(3):
                        last = nc.tensor.transpose(ps_p[:, n, :], pick[:, n, :], ident[:])
                    last.then_inc(s("picks_turned"), 1)
                    for k in range(NBATCH):
                        pe.wait_ge(s("onehot"), NBATCH * t + k + 1)
                        pe.wait_ge(s("oh1"), NBATCH * t + k + 1)
                        if k < 2:
                            pe.wait_ge(s("gates_read1"), (NBATCH // 2) * t)
                        else:
                            blk = (k - 2) // (NBATCH // 2)
                            pe.wait_ge(s(f"gates_read{blk}"), (NBATCH // 2) * t + (k - 2) % (NBATCH // 2) + 1)
                        for n in range(OB):
                            last = nc.tensor.matmul(ps_w[k % 2][:, n, :], o1[k % 2][:, n, :], o2[k % 2][:, n, :],
                                                    start=True, stop=True)
                        last.then_inc(s(f"gates_mm{k % 2}"), 1)
                run(pe, 0, NT, step)

        s.clear()

        with ExitStack() as c6:
            acc = sb(c6, "acc", [P, NT, D])
            with ExitStack() as c:
                v_raw = sb(c, "v_raw", [P, VG, D])
                v_hi = [sb(c, f"v_hi{b}", [P, VG, D], F32R) for b in (0, 1)]
                v_lo = [sb(c, f"v_lo{b}", [P, VG, D], F32R) for b in (0, 1)]
                w_raw = [sb(c, f"w_raw{b}", [P, N // WB, VG * WB]) for b in (0, 1)]
                ga = sb(c, "ga", [P, VG, N])
                a_hi = sb(c, "a_hi", [P, 2, VG, N], F32R)
                a_lo = sb(c, "a_lo", [P, 2, VG, N], F32R)
                banks = [pb(c, f"u_ps{b}", [P, 2, 512]) for b in (0, 1)]
                ps_y = [pb(c, f"y_ps{b}", [P, 512]) for b in range(4)]
                lin = Linear(c, "u", a["u"], NK, banks)
                v_rows = a["v"]
                body = 2 * VG
                npass = NK // body
                block = c.enter_context(nc.Block())

                @block.sync
                def _(sp):
                    def step(i):
                        for gp in (0, 1):
                            sp.wait_ge(s(f"mult{gp}"), VG * i)
                            sp.dma_start(w_raw[gp][:], wgt_d[:, :, bass.ds((2 * i + gp) * VG * WB, VG * WB)]
                                         ).then_inc(s(f"ld_w{gp}"), 16)
                            for c_ in range(VG):
                                lin.load(sp, VG * i + (VG * gp + c_) // 2, c_ % 2)
                                if c_ == 0:
                                    sp.wait_ge(s("v_split"), VG * (2 * i + gp))
                                    sp.dma_start(v_raw[:, :, :].rearrange("p c d -> p (c d)"),
                                                 v_rows[:, bass.ds((2 * i + gp) * VG * D, VG * D)]
                                                 ).then_inc(s("ld_v"), 16)
                    run(sp, 0, npass, step)

                @block.scalar
                def _(act):
                    def gelu(i, m):
                        lin.wait_out(act, VG * i + m // 2, m % 2)
                        act.wait_ge(s("a_split"), body * i + max(m - VG + 1, 0))
                        nc.scalar.activation(halves(ga[:, m % VG, :]), lin.out(m % 2), ACT.Gelu_apprx_tanh
                                             ).then_inc(lin.sem("evac", m % 2), 1)

                    def head_a(i, m):
                        act.wait_ge(s(f"mult{m // VG}"), VG * i + m % VG + 1)
                        nc.scalar.activation(a_hi[:, m // VG, m % VG, :], ga[:, m % VG, :], ACT.Copy
                                             ).then_inc(s("a_head"), 1)
                    def step(i):
                        for m in range(body + 2):
                            if m < body:
                                gp, c_ = m // VG, m % VG
                                lin.head(act, VG * i + m // 2, m % 2)
                                act.wait_ge(s("ld_v"), 16 * (2 * i + gp) + 16)
                                act.wait_ge(s(f"y_mm{gp}"), 2 * NT * i)
                                nc.scalar.activation(v_hi[gp][:, c_, :], v_raw[:, c_, :], ACT.Copy
                                                     ).then_inc(s("v_head"), 1)
                            if 1 <= m <= body:
                                gelu(i, m - 1)
                            if m >= 2:
                                head_a(i, m - 2)
                    run(act, 0, npass, step)

                @block.gpsimd
                def _(pool):
                    def step(i):
                        for m in range(body):
                            gp, c_ = m // VG, m % VG
                            lin.rest(pool, VG * i + m // 2, m % 2)
                            pool.wait_ge(s("v_head"), body * i + m + 1)
                            nc.gpsimd.tensor_tensor(v_lo[gp][:, c_, :], v_raw[:, c_, :], v_hi[gp][:, c_, :].bitcast(F32),
                                                    ALU.subtract).then_inc(s("v_split"), 1)
                    run(pool, 0, npass, step)

                @block.vector
                def _(dve):
                    nc.vector.memset(acc[:], 0.0).then_inc(s("acc0"), 1)
                    dve.wait_ge(s("acc0"), 1)
                    def step(i):
                        for m in range(body):
                            gp, c_ = m // VG, m % VG
                            dve.wait_ge(lin.sem("evac", m % 2), VG * i + m // 2 + 1)
                            if c_ == 0:
                                dve.wait_ge(s(f"ld_w{gp}"), 16 * i + 16)
                            col = ga[:, c_, :].rearrange("p (b n) -> p b n", n=WB)
                            nc.vector.tensor_tensor(col, col, w_raw[gp][:, :, c_ * WB:c_ * WB + WB], ALU.mult
                                                    ).then_inc(s(f"mult{gp}"), 1)
                            dve.wait_ge(s("a_head"), body * i + m + 1)
                            nc.vector.tensor_tensor(a_lo[:, gp, c_, :], ga[:, c_, :], a_hi[:, gp, c_, :].bitcast(F32),
                                                    ALU.subtract).then_inc(s("a_split"), 1)
                        for gp in (0, 1):
                            for r in range(2 * NT):
                                q = 2 * NT * gp + r
                                dve.wait_ge(s(f"y_mm{gp}"), 2 * NT * i + r + 1)
                                part_ = acc[:, r // 2, (r % 2) * 512:(r % 2) * 512 + 512]
                                nc.vector.tensor_tensor(part_, part_, ps_y[q % 4][:, :], ALU.add
                                                        ).then_inc(s(f"y_add{q % 4}"), 1)
                    run(dve, 0, npass, step)

                @block.tensor
                def _(pe):
                    def step(i):
                        for m in range(body):
                            lin.product(pe, VG * i + m // 2, m % 2)
                        for gp in (0, 1):
                            pe.wait_ge(s("a_split"), body * i + VG * gp + VG)
                            pe.wait_ge(s("v_split"), body * i + VG * gp + VG)
                            for r in range(2 * NT):
                                q = 2 * NT * gp + r
                                ts = slice((r // 2) * P, (r // 2) * P + P)
                                ds_ = slice((r % 2) * 512, (r % 2) * 512 + 512)
                                pe.wait_ge(s(f"y_add{q % 4}"), 5 * i + q // 4)
                                for c_ in range(VG):
                                    hi, lo = a_hi[:, gp, c_, ts], a_lo[:, gp, c_, ts]
                                    nc.tensor.matmul(ps_y[q % 4][:, :], hi, v_hi[gp][:, c_, ds_], start=(c_ == 0), stop=False)
                                    nc.tensor.matmul(ps_y[q % 4][:, :], hi, v_lo[gp][:, c_, ds_], start=False, stop=False)
                                    last = nc.tensor.matmul(ps_y[q % 4][:, :], lo, v_hi[gp][:, c_, ds_],
                                                            start=False, stop=(c_ == VG - 1))
                                last.then_inc(s(f"y_mm{gp}"), 1)
                    run(pe, 0, npass, step)

            with ExitStack() as c:
                x2 = [sb(c, f"x2_{k}", [P, D]) for k in range(NT)]
                nf = sb(c, "nf", [P, D])
                ones = sb(c, "ones", [P, P])
                g2row = sb(c, "g2row", [P, 2, D])
                diag = sb(c, "diag", [P, 2 * KC, P])
                sqs = sb(c, "sqs", [P, D])
                st = sb(c, "st", [P, 5, NT])
                ps_g = pb(c, "ps_g", [P, 4, 512])
                block = c.enter_context(nc.Block())

                @block.sync
                def _(sp):
                    sp.dma_start(ones[:], a["ones"]).then_inc(s("ld_ones"), 16)
                    sp.dma_start(nf[:], a["norm_final"]).then_inc(s("ld7"), 16)
                    for k in range(NT):
                        sp.dma_start(x2[k][:], x2_d[k]).then_inc(s("ld7"), 16)
                    for k in range(NT):
                        sp.wait_ge(s("final"), k + 1)
                        dst = y_prompt if k == 0 else y_sample[(k - 1) * P:k * P, :]
                        sp.dma_start(dst, x2[k][:]).then_inc(s("st_y"), 16)
                    sp.wait_ge(s("st_y"), 16 * NT)

                @block.scalar
                def _(act):
                    for k in range(NT):
                        act.wait_ge(s("resid"), k + 1)
                        nc.scalar.activation(sqs[:], x2[k][:], ACT.Square, accum_out=st[:, 0, k:k + 1]
                                             ).then_inc(s("ssq"), 1)
                        act.wait_ge(s("ssq"), k + 1)
                    act.wait_ge(s("fin_var"), 1)
                    nc.scalar.activation(st[:, 2, :], st[:, 1, :], ACT.Sqrt).then_inc(s("fin_root"), 1)

                @block.vector
                def _(dve):
                    link = Chain(dve, s("dve7"))
                    V = nc.vector
                    for k in range(2 * KC):
                        V.tensor_scalar(diag[:, k, :], ident[:], mod[:, 5 * KC + k % KC, k // KC:k // KC + 1], None,
                                        ALU.mult).then_inc(s("diag"), 1)
                    for k in range(4):
                        dve.wait_ge(s("g2_ps"), k + 1)
                        link(V.tensor_copy(g2row[:, k // 2, (k % 2) * 512:(k % 2) * 512 + 512], ps_g[:, k, :]))
                    dve.wait_ge(s("ld7"), 16 * (NT + 1))
                    for k in range(NT):
                        link(V.tensor_tensor(acc[:, k, :], acc[:, k, :], g2row[:, min(k, 1), :], ALU.mult))
                        V.tensor_tensor(x2[k][:], x2[k][:], acc[:, k, :], ALU.add).then_inc(s("resid"), 1)
                    dve.wait_ge(s("ssq"), NT)
                    link(V.tensor_scalar(st[:, 0, :], st[:, 0, :], 1.0 / D, None, ALU.mult))
                    rstd_ops(dve, link, "fin", st[:, 0, :], st[:, 1, :], st[:, 1, :], st[:, 2, :], st[:, 3, :], st[:, 4, :])
                    for k in range(NT):
                        V.scalar_tensor_tensor(out=x2[k][:], in0=x2[k][:], scalar=st[:, 3, k:k + 1], in1=nf[:],
                                               op0=ALU.mult, op1=ALU.mult).then_inc(s("final"), 1)

                @block.tensor
                def _(pe):
                    pe.wait_ge(s("ld_ones"), 16)
                    for k in range(2 * KC):
                        pe.wait_ge(s("diag"), k + 1)
                        last = nc.tensor.matmul(ps_g[:, k // 4, (k % 4) * P:(k % 4) * P + P], ones[:], diag[:, k, :],
                                                start=True, stop=True)
                        if k % 4 == 3:
                            last.then_inc(s("g2_ps"), 1)


def layout(x):
    c = np.ascontiguousarray

    def columns(v):
        return np.asarray(v).reshape(-1, P).T

    def slabs(w, cols=None):
        w = np.asarray(w)
        w = w if cols is None else w[:, cols]
        k, m = w.shape
        return c(w.reshape(k // P, P, m // P, P).transpose(2, 1, 0, 3).reshape(m // P, P, k))

    x = {k: np.asarray(v) for k, v in x.items()}
    tokens = np.concatenate([x["x_prompt"][0], x["x_sample"][0]], 0)
    r = np.arange
    swapped = np.concatenate([r(ROPE // 2, ROPE), r(0, ROPE // 2)])
    kr0 = 384
    kr = np.concatenate([kr0 + r(ROPE), kr0 + swapped] * 2)
    order = np.concatenate([r(0, kr0), kr, r(kr0 + ROPE, x["w_in"].shape[2])])
    qh = r(HEADS)[:, None] * QK
    uq = x["w_uq"][0][:, np.concatenate([(qh + r(NOPE)).ravel(), (qh + NOPE + r(ROPE)).ravel(),
                                         (qh + NOPE + swapped).ravel()])]
    kh = r(HEADS)[:, None] * (NOPE + VD)
    ukv = x["w_ukv"][0][:, np.concatenate([(kh + r(NOPE)).ravel(), (kh + NOPE + r(VD)).ravel()])]
    out = {
        "x_t": tokens.T.reshape(KC, P, N).transpose(1, 0, 2),
        "cvec": np.stack([columns(x["c_ctx"]), columns(x["c"][0])], 2),
        "w_mod": slabs(x["w_mod"][0]), "bmod": columns(x["b_mod"][0]),
        "cols": np.concatenate([columns(x["norm_mix"][0]), columns(x["norm_ffn"][0]), columns(x["q_norm"][0]),
                                columns(x["kv_norm"][0]), columns(x["ret_gn"][0]),
                                np.tile(np.concatenate([x["ret_logit_fwd"][0], x["ret_logit_bwd"][0]]), (P, 1)),
                                np.tile(x["c_ctx"][:9], (P, 1))], 1),
        "w_in": slabs(x["w_in"][0], order),
        "w_uq": uq.reshape(2, P, D).transpose(1, 0, 2), "w_ukv": ukv.reshape(P, 2, 512),
        "cache_ckv_t": x["cache_ckv"][0, 0].T, "cache_kr_t": x["cache_krope"][0, 0].T,
        "state": np.stack([x["state_ret_fwd"][0, 0], x["state_ret_bwd"][0, 0]]).transpose(2, 0, 1, 3),
        "w_up": slabs(np.concatenate([x["w_up_a"][0], x["w_up_b"][0]], 0)),
        "w_o": slabs(x["w_o"][0]), "w_q": slabs(x["peer_wq"][0]),
        "keys_t": np.stack([x["peer_keys1"][0], x["peer_keys2"][0]], 1).reshape(16, NK, P).transpose(2, 0, 1),
        "u": x["peer_u"][0].reshape(NK, NK, KC, P).transpose(1, 3, 2, 0).reshape(NK, P, D),
        "v": x["peer_v"][0].reshape(NK, NK * D),
        "norm_final": np.tile(x["norm_final"], (P, 1)),
    }
    out.update(constants())
    return {k: c(v) for k, v in out.items()}


def constants():
    f = np.float32
    pos = np.arange(NLAT)
    freqs = np.power(f(ROPE_BASE), -np.arange(ROPE // 4, dtype=f) / f(ROPE // 4)).astype(f)
    ang = np.concatenate([(pos // GRID_W).astype(f)[:, None] * freqs, (pos % GRID_W).astype(f)[:, None] * freqs], 1)
    cos, sin = np.cos(ang).T.astype(f), np.sin(ang).T.astype(f)
    diff = (np.arange(NLAT + 384) - 384)[None, :] - np.arange(P)[:, None]
    p = np.arange(P, dtype=f)[:, None]
    full = lambda v: np.full((P, P), v, f)
    return {
        "cos_t": np.tile(np.concatenate([cos, cos], 0), (4, 1)), "sin_t": np.tile(np.concatenate([-sin, sin], 0), (4, 1)),
        "ident": np.eye(P, dtype=f), "ones": full(1.0), "inv_d": full(1.0 / D), "inv_q": full(1.0 / 256),
        "inv_k": full(1.0 / P),
        "rel0": np.maximum(diff, 0).astype(f), "rel1": np.maximum(-diff, 0).astype(f),
        "msk0": (diff >= 0).astype(f), "msk1": (diff <= 0).astype(f),
        "steps": np.tile(np.stack([np.arange(1, NLAT + 1), np.arange(NLAT, 0, -1)]).astype(f)[None], (P, 1, 1)),
        "ksteps": np.concatenate([np.repeat(P - 1 - p, RH, 1), np.repeat(p, RH, 1)], 1),
        "iota_r": np.tile(np.arange(NK, dtype=f), (P, 1)),
    }


OUTS = [("y_prompt", (NCTX, D)), ("y_sample", (NLAT, D)), ("new_ckv", (NCTX, 128)), ("new_kr", (NCTX, ROPE)),
        ("new_sf", (DK, RH, DK)), ("new_sb", (DK, RH, DK))]


def kernel(**inputs):
    import concourse.bacc as bacc
    from concourse.bass_utils import run_bass_kernel_spmd

    nc = bacc.Bacc("TRN2", target_bir_lowering=False, num_devices=1)
    arrays = layout(inputs)
    aps = {k: nc.dram_tensor(k + "_dram", v.shape, F32, kind="ExternalInput").ap() for k, v in arrays.items()}
    outs = [nc.dram_tensor(n + "_dram", shape, F32, kind="ExternalOutput").ap() for n, shape in OUTS]
    build(nc, aps, outs)
    result = run_bass_kernel_spmd(nc, [{k + "_dram": v for k, v in arrays.items()}], core_ids=[0])
    got = {n: result.results[0][n + "_dram"] for n, _ in OUTS}
    return (got["y_prompt"][None], got["y_sample"][None], got["new_ckv"][None, None], got["new_kr"][None, None],
            got["new_sf"].transpose(1, 0, 2)[None, None], got["new_sb"].transpose(1, 0, 2)[None, None])
```

```python
from contextlib import ExitStack

import numpy as np

import concourse.bass as bass
from concourse import mybir

F32 = mybir.dt.float32
F32R = mybir.dt.float32r
U32 = mybir.dt.uint32
ACT = mybir.ActivationFunctionType
ALU = mybir.AluOpType
AX = mybir.AxisListType

P = 128
D = 1024
KC = D // P
NCTX, NLAT = 128, 512
N = NCTX + NLAT
NT = N // P
NH2 = N // 2
PAST = 128
NALL = N + PAST
EPS = 1e-6
HEADS, NOPE, ROPE, VD = 8, 64, 32, 64
QK = NOPE + ROPE
ATT_SCALE = QK ** -0.5
RH, DK = 4, 128
RET_SCALE = DK ** -0.5
PH, TOPK = 8, 16
PICKS = PH * TOPK
NK = 128
NMOD = 6 * KC
M_CQ, M_CKV, M_KR, M_RQ, M_RK, M_RV, M_RG, M_GATE, M_END = 0, 2, 3, 4, 8, 12, 16, 20, 36
GRID_W, ROPE_BASE = 64, 10000.0
LOW = -3.0e38
WB = 64
OB = 8
VG = 4
VGROUPS = NK // VG


class Sems:

    def __init__(self, nc):
        self.nc, self.made = nc, {}

    def __call__(self, name):
        if name not in self.made:
            self.made[name] = self.nc.alloc_semaphore(name=name)
        return self.made[name]

    def clear(self):
        self.nc.all_engine_barrier()
        self.nc.clear_and_free_semaphores(list(self.made.values()))
        self.nc.all_engine_barrier()
        self.made = {}


def run(eng, first, end, step):
    step(first)
    with eng.Fori(first + 1, end) as i:
        step(i)


class Chain:

    def __init__(self, eng, sem):
        self.eng, self.sem, self.n = eng, sem, 0

    def __call__(self, ins):
        self.n += 1
        ins.then_inc(self.sem, 1)
        self.eng.wait_ge(self.sem, self.n)


def build(nc, a, outs):
    y_prompt, y_sample, new_ckv, new_kr, new_sf, new_sb = outs
    gates_d = nc.dram_tensor("gates_scratch", (16, P, N), F32, kind="Internal").ap()
    scores_d = nc.dram_tensor("scores_scratch", (NT, P, 16 * NK), F32, kind="Internal").ap()
    x2_d = nc.dram_tensor("x2_scratch", (NT, P, D), F32, kind="Internal").ap()
    act_d = nc.dram_tensor("act_scratch", (NK, P, N), F32, kind="Internal").ap()
    wgt_d = nc.dram_tensor("wgt_scratch", (P, N // WB, NK * WB), F32, kind="Internal").ap()

    with ExitStack() as top:
        s = Sems(nc)

        def sb(ctx, name, shape, dt=F32):
            return ctx.enter_context(nc.sbuf_tensor(name, shape, dt))

        def pb(ctx, name, shape, dt=F32):
            return ctx.enter_context(nc.psum_tensor(name, shape, dt))

        mod = sb(top, "mod", [P, NMOD, 2])
        cols = sb(top, "cols", [P, 40])
        ident = sb(top, "ident", [P, P])
        hidden = top.enter_context(ExitStack())
        h_hi = sb(hidden, "h_hi", [P, KC, N], F32R)
        h_lo = sb(hidden, "h_lo", [P, KC, N], F32R)

        class Linear:

            def __init__(self, ctx, tag, w_dram, count, banks):
                self.tag, self.w, self.count, self.ps = tag, w_dram, count, banks
                self.raw = [sb(ctx, f"{tag}_raw{b}", [P, KC, P]) for b in (0, 1)]
                self.hi = [sb(ctx, f"{tag}_hi{b}", [P, KC, P], F32R) for b in (0, 1)]
                self.lo = [sb(ctx, f"{tag}_lo{b}", [P, KC, P], F32R) for b in (0, 1)]

            def sem(self, what, b):
                return s(f"{self.tag}_{what}{b}")

            def load(self, sp, pair, b):
                sp.wait_ge(self.sem("split", b), pair)
                sp.dma_start(self.raw[b][:, :, :].rearrange("p k m -> p (k m)"),
                             self.w[bass.ds(2 * pair + b, 1)].rearrange("o p m -> p (o m)")
                             ).then_inc(self.sem("loaded", b), 16)

            def head(self, act, pair, b):
                act.wait_ge(self.sem("loaded", b), 16 * pair + 16)
                act.wait_ge(self.sem("product", b), pair)
                nc.scalar.activation(self.hi[b][:], self.raw[b][:], ACT.Copy).then_inc(self.sem("head", b), 1)

            def rest(self, pool, pair, b):
                pool.wait_ge(self.sem("head", b), pair + 1)
                nc.gpsimd.tensor_tensor(self.lo[b][:], self.raw[b][:], self.hi[b][:].bitcast(F32),
                                        ALU.subtract).then_inc(self.sem("split", b), 1)

            def product(self, pe, pair, b, groups=((0, KC),)):
                pe.wait_ge(self.sem("split", b), pair + 1)
                pe.wait_ge(self.sem("evac", b), pair)
                for g, (k0, k1) in enumerate(groups):
                    for half in (0, 1):
                        cs = slice(half * NH2, half * NH2 + NH2)
                        out = self.ps[b][:, 2 * g + half, 0:NH2]
                        for kc in range(k0, k1):
                            nc.tensor.matmul(out, self.hi[b][:, kc, :], h_hi[:, kc, cs],
                                             start=(kc == k0), stop=False)
                            nc.tensor.matmul(out, self.hi[b][:, kc, :], h_lo[:, kc, cs],
                                             start=False, stop=False)
                            last = nc.tensor.matmul(out, self.lo[b][:, kc, :], h_hi[:, kc, cs],
                                                    start=False, stop=(kc == k1 - 1))
                last.then_inc(self.sem("product", b), 1)

            def wait_out(self, eng, pair, b):
                eng.wait_ge(self.sem("product", b), pair + 1)

            def out(self, b, g=0):
                return self.ps[b][:, 2 * g:2 * g + 2, 0:NH2]

        def halves(ap):
            return ap.rearrange("p (h n) -> p h n", h=2)

        def rstd_ops(dve, link, tag, mean_sq, var_out, var, root, r, t):
            nc.vector.tensor_scalar(var_out, mean_sq, EPS, None, ALU.add).then_inc(s(tag + "_var"), 1)
            dve.wait_ge(s(tag + "_root"), 1)
            link(nc.vector.reciprocal(r, root))
            link(nc.vector.tensor_tensor(t, r, r, ALU.mult))
            link(nc.vector.tensor_tensor(t, t, var, ALU.mult))
            link(nc.vector.tensor_scalar(t, t, -0.5, 1.5, ALU.mult, ALU.add))
            link(nc.vector.tensor_tensor(r, r, t, ALU.mult))

        C_MIX, C_FFN, C_QN, C_KVN, C_GN, C_LOG = 0, 8, 16, 18, 19, 23

        with ExitStack() as mixer:
            x_t = sb(mixer, "x_t", [P, KC, N])
            act_buf = sb(mixer, "act_buf", [P, KC, N])
            gscale = sb(mixer, "gscale", [P, KC, 2])

            def norm_pe(pe, tag, src, inv_in, ps, sq_sem):
                for kc in range(KC):
                    pe.wait_ge(s(sq_sem), kc + 1)
                    for half in (0, 1):
                        last = nc.tensor.matmul(ps[:, half, 0:NH2], inv_in[:],
                                                src[:, kc, half * NH2:half * NH2 + NH2],
                                                start=(kc == 0), stop=(kc == KC - 1))
                last.then_inc(s(tag + "_meansq"), 1)

            def norm_dve(dve, link, tag, ps, wrk, c_norm, m_shift, m_scale):
                var, root, r, t = wrk
                for g in (0, 1):
                    link(nc.vector.scalar_tensor_tensor(
                        out=gscale[:, :, g], in0=mod[:, m_scale:m_scale + KC, g], scalar=1.0,
                        in1=cols[:, c_norm:c_norm + KC], op0=ALU.add, op1=ALU.mult))
                dve.wait_ge(s(tag + "_meansq"), 1)

                rstd_ops(dve, link, tag, ps[:, :, 0:NH2], halves(var[:, :]), var[:, :], root[:, :], r[:, :], t[:, :])
                for kc in range(KC):
                    link(nc.vector.tensor_tensor(act_buf[:, kc, :], x_t[:, kc, :], r[:, :], ALU.mult))
                    for g, cs in ((0, slice(0, NCTX)), (1, slice(NCTX, N))):
                        ins = nc.vector.tensor_scalar(
                            act_buf[:, kc, cs], act_buf[:, kc, cs], gscale[:, kc, g:g + 1],
                            mod[:, m_shift + kc, g:g + 1], ALU.mult, ALU.add)
                        ins.then_inc(s(tag + "_h"), 1)
                for kc in range(KC):
                    dve.wait_ge(s(tag + "_hi"), kc + 1)
                    nc.vector.tensor_tensor(h_lo[:, kc, :], act_buf[:, kc, :],
                                            h_hi[:, kc, :].bitcast(F32), ALU.subtract
                                            ).then_inc(s(tag + "_split"), 1)

            def norm_act(act, tag, wrk):
                var, root, r, t = wrk
                act.wait_ge(s(tag + "_var"), 1)
                nc.scalar.activation(root[:, :], var[:, :], ACT.Sqrt).then_inc(s(tag + "_root"), 1)
                for kc in range(KC):
                    act.wait_ge(s(tag + "_h"), 2 * kc + 2)
                    nc.scalar.activation(h_hi[:, kc, :], act_buf[:, kc, :], ACT.Copy
                                         ).then_inc(s(tag + "_hi"), 1)

            with ExitStack() as keep:
                proj = sb(keep, "proj", [P, M_GATE, N])

                with ExitStack() as c1:
                    wm = [sb(c1, f"wm{b}", [P, KC, P]) for b in (0, 1)]
                    cvec = sb(c1, "cvec", [P, KC, 2])
                    csil = sb(c1, "csil", [P, KC, 2])
                    bmod = sb(c1, "bmod", [P, NMOD])
                    inv_d = sb(c1, "inv_d", [P, P])
                    wrk = [sb(c1, f"n1_{n}", [P, N]) for n in ("var", "root", "r", "t")]
                    gate = [sb(c1, f"gate{b}", [P, N]) for b in (0, 1)]
                    ps_mod = pb(c1, "ps_mod", [P, NMOD, 2])
                    ps_n = pb(c1, "ps_n", [P, 2, 512])
                    banks = [pb(c1, f"win_ps{b}", [P, 2, 512]) for b in (0, 1)]
                    lin = Linear(c1, "win", a["w_in"], M_END, banks)
                    npair = M_END // 2
                    gpair = M_GATE // 2
                    block = c1.enter_context(nc.Block())

                    @block.sync
                    def _(sp):
                        for dst, name in ((cvec[:], "cvec"), (bmod[:], "bmod"), (cols[:], "cols"),
                                          (x_t[:], "x_t"), (ident[:], "ident"),
                                          (inv_d[:], "inv_d")):
                            sp.dma_start(dst, a[name]).then_inc(s("ld_" + name), 16)
                        def step(i):
                            for b in (0, 1):
                                sp.wait_ge(s(f"wm_used{b}"), i)
                                sp.dma_start(wm[b][:, :, :].rearrange("p k m -> p (k m)"),
                                             a["w_mod"][bass.ds(2 * i + b, 1)].rearrange("o p m -> p (o m)")
                                             ).then_inc(s(f"wm_ld{b}"), 16)
                        run(sp, 0, NMOD // 2, step)
                        def step(i):
                            for b in (0, 1):
                                lin.load(sp, i, b)
                        run(sp, 0, npair, step)
                        for b in (0, 1):
                            sp.wait_ge(s(f"gate_st{b}"), 16 * (npair - gpair))

                    @block.scalar
                    def _(act):
                        act.wait_ge(s("ld_cvec"), 16)
                        nc.scalar.activation(csil[:], cvec[:], ACT.Silu).then_inc(s("csil"), 1)
                        act.wait_ge(s("ld_x_t"), 16)
                        for kc in range(KC):
                            nc.scalar.activation(act_buf[:, kc, :], x_t[:, kc, :], ACT.Square
                                                 ).then_inc(s("n1_sq"), 1)
                        norm_act(act, "n1", wrk)
                        def step(i):
                            for b in (0, 1):
                                lin.head(act, i, b)
                        run(act, 0, gpair, step)
                        def step(i):
                            for b in (0, 1):
                                lin.head(act, i, b)
                                lin.wait_out(act, i, b)
                                act.wait_ge(s(f"gate_st{b}"), 16 * (i - gpair))
                                nc.scalar.activation(halves(gate[b][:, :]), lin.out(b), ACT.Sigmoid
                                                     ).then_inc(lin.sem("evac", b), 1)
                                act.wait_ge(lin.sem("evac", b), i + 1)
                                act.dma_start(gates_d[bass.ds(2 * (i - gpair) + b, 1)].rearrange("o p m -> p (o m)"),
                                              gate[b][:]).then_inc(s(f"gate_st{b}"), 16)
                        run(act, gpair, npair, step)

                    @block.gpsimd
                    def _(pool):
                        def step(i):
                            for b in (0, 1):
                                lin.rest(pool, i, b)
                        run(pool, 0, npair, step)

                    @block.vector
                    def _(dve):
                        link = Chain(dve, s("dve1"))
                        dve.wait_ge(s("wm_used1"), NMOD // 2)
                        dve.wait_ge(s("ld_bmod"), 16)
                        dve.wait_ge(s("ld_cols"), 16)
                        for g in (0, 1):
                            link(nc.vector.tensor_tensor(mod[:, :, g], ps_mod[:, :, g], bmod[:, :], ALU.add))
                        norm_dve(dve, link, "n1", ps_n, wrk, C_MIX, 0, KC)
                        def step(i):
                            for b in (0, 1):
                                lin.wait_out(dve, i, b)
                                nc.vector.tensor_copy(
                                    proj[:, bass.ds(2 * i + b, 1), :].rearrange("p o (h n) -> p (o h) n", h=2),
                                    lin.out(b)).then_inc(lin.sem("evac", b), 1)
                        run(dve, 0, gpair, step)

                    @block.tensor
                    def _(pe):
                        pe.wait_ge(s("csil"), 1)
                        pe.wait_ge(s("ld_inv_d"), 16)
                        norm_pe(pe, "n1", act_buf, inv_d, ps_n, "n1_sq")
                        def step(i):
                            for b in (0, 1):
                                pe.wait_ge(s(f"wm_ld{b}"), 16 * i + 16)
                                for kc in range(KC):
                                    last = nc.tensor.matmul(
                                        ps_mod[:, bass.ds(2 * i + b, 1), :].rearrange("p o g -> p (o g)"),
                                        wm[b][:, kc, :], csil[:, kc, :], start=(kc == 0), stop=(kc == KC - 1))
                                last.then_inc(s(f"wm_used{b}"), 1)
                        run(pe, 0, NMOD // 2, step)
                        pe.wait_ge(s("n1_split"), KC)
                        def step(i):
                            for b in (0, 1):
                                lin.product(pe, i, b)
                        run(pe, 0, npair, step)

                with ExitStack() as c2:
                    w_uq = sb(c2, "w_uq", [P, 2, D])
                    w_ukv = sb(c2, "w_ukv", [P, 2, 512])
                    cos_t = sb(c2, "cos_t", [P, NLAT])
                    sin_t = sb(c2, "sin_t", [P, NLAT])
                    inv_q = sb(c2, "inv_q", [P, P])
                    inv_k = sb(c2, "inv_k", [P, P])
                    q_h = sb(c2, "q_h", [QK, HEADS, N])
                    k_h = sb(c2, "k_h", [QK, HEADS, NALL])
                    ckv = sb(c2, "ckv", [P, NALL])
                    v_tok = sb(c2, "v_tok", [P, NALL // P, 512])
                    kr_past = sb(c2, "kr_past", [ROPE, PAST])
                    kr_new = act_buf[0:ROPE, 7, :]
                    probs = [act_buf[:, 0, :], act_buf[:, 7, :]]
                    probs_t = [act_buf[:, 1, :], act_buf[:, 2, :]]
                    stat = [sb(c2, f"stat{b}", [P, 4]) for b in (0, 1)]
                    ckv_out = act_buf[:, 3, 0:P + ROPE]
                    sq = act_buf[:, 0, :]
                    var, root, r, t = (act_buf[:, k, :] for k in (1, 2, 3, 4))
                    t1, t2 = act_buf[:, 5, 0:NLAT], act_buf[:, 6, 0:NLAT]
                    sqb = act_buf[:, 7, :]
                    ps_s = [pb(c2, f"ps_s{b}", [P, 2, 512]) for b in (0, 1)]
                    ps_t = pb(c2, "ps_t", [P, 2, 512])
                    ps_o = [pb(c2, f"ps_o{b}", [P, 512]) for b in (0, 1)]
                    units = [(qt, h) for qt in range(NT) for h in range(HEADS)]

                    def keys(qt):
                        return [0] if qt == 0 else list(range(1, NALL // P))
                    block = c2.enter_context(nc.Block())

                    @block.sync
                    def _(sp):
                        for dst, name in ((w_uq[:], "w_uq"), (w_ukv[:], "w_ukv"), (cos_t[:], "cos_t"),
                                          (sin_t[:], "sin_t"), (inv_q[:], "inv_q"), (inv_k[:], "inv_k"),
                                          (ckv[:, N:NALL], "cache_ckv_t"), (kr_past[:], "cache_kr_t")):
                            sp.dma_start(dst, a[name]).then_inc(s("ld_" + name), 16)
                        sp.wait_ge(s("ckv_out"), 2)
                        sp.dma_start(new_ckv, ckv_out[:, 0:P]).then_inc(s("st_kv"), 16)
                        sp.dma_start(new_kr, ckv_out[:, P:P + ROPE]).then_inc(s("st_kv"), 16)
                        sp.wait_ge(s("st_kv"), 32)

                    @block.scalar
                    def _(act):
                        for i, m in enumerate((M_CQ, M_CQ + 1, M_CKV)):
                            if i == 2:
                                act.wait_ge(s("cq_meansq"), 1)
                            dst = sqb if i == 1 else sq
                            nc.scalar.activation(dst, proj[:, m, :], ACT.Square).then_inc(s("lat_sq"), 1)
                            if i == 1:
                                act.wait_ge(s("cq_var"), 1)
                                nc.scalar.activation(root, var, ACT.Sqrt).then_inc(s("cq_root"), 1)
                        act.wait_ge(s("ckv_var"), 1)
                        nc.scalar.activation(root, var, ACT.Sqrt).then_inc(s("ckv_root"), 1)
                        act.wait_ge(s("kr_done"), 1)
                        act.wait_ge(s("ld_cache_kr_t"), 16)
                        for h in range(HEADS):
                            nc.scalar.activation(k_h[NOPE:QK, h, 0:N], kr_new, ACT.Copy).then_inc(s("kh_rope"), 1)
                            nc.scalar.activation(k_h[NOPE:QK, h, N:NALL], kr_past[:], ACT.Copy).then_inc(s("kh_rope"), 1)
                        for u, (qt, h) in enumerate(units):
                            b, nk = u % 2, len(keys(qt)) * P
                            act.wait_ge(s("negmax"), u + 1)
                            if u >= 2:
                                act.wait_ge(s("turned"), u - 1)
                            src = ps_s[b][:, 0, 0:P] if qt == 0 else ps_s[b][:, :, 0:NH2]
                            dst = probs[b][:, 0:nk] if qt == 0 else halves(probs[b])
                            nc.scalar.activation(dst, src, ACT.Exp, bias=stat[b][:, 1:2], scale=ATT_SCALE,
                                                 accum_out=stat[b][:, 2:3]).then_inc(s("exp"), 1)

                    @block.vector
                    def _(dve):
                        link = Chain(dve, s("dve2"))
                        dve.wait_ge(s("cq_meansq"), 1)
                        rstd_ops(dve, link, "cq", ps_s[0][:, :, 0:NH2], halves(var), var, root, r, t)
                        for k in (0, 1):
                            ins = nc.vector.scalar_tensor_tensor(
                                out=proj[:, M_CQ + k, :], in0=proj[:, M_CQ + k, :],
                                scalar=cols[:, C_QN + k:C_QN + k + 1], in1=r, op0=ALU.mult, op1=ALU.mult)
                            ins.then_inc(s("cq_normed"), 1)
                        dve.wait_ge(s("cq_normed"), 2)
                        dve.wait_ge(s("ckv_meansq"), 1)
                        rstd_ops(dve, link, "ckv", ps_s[1][:, :, 0:NH2], halves(var), var, root, r, t)
                        nc.vector.scalar_tensor_tensor(
                            out=ckv[:, 0:N], in0=proj[:, M_CKV, :], scalar=cols[:, C_KVN:C_KVN + 1],
                            in1=r, op0=ALU.mult, op1=ALU.mult).then_inc(s("ckv_normed"), 1)
                        dve.wait_ge(s("ld_cos_t"), 16)
                        dve.wait_ge(s("ld_sin_t"), 16)
                        link(nc.vector.tensor_copy(kr_new[:, 0:NCTX], proj[0:ROPE, M_KR, 0:NCTX]))
                        link(nc.vector.tensor_tensor(t1[0:ROPE], proj[0:ROPE, M_KR, NCTX:N], cos_t[0:ROPE, :], ALU.mult))
                        link(nc.vector.tensor_tensor(t2[0:ROPE], proj[ROPE:2 * ROPE, M_KR, NCTX:N],
                                                     sin_t[ROPE:2 * ROPE, :], ALU.mult))
                        nc.vector.tensor_tensor(kr_new[:, NCTX:N], t1[0:ROPE], t2[0:ROPE], ALU.add
                                                ).then_inc(s("kr_done"), 1)
                        dve.wait_ge(s("ctx_turned"), 1)
                        nc.vector.tensor_copy(ckv_out[:, 0:P], ps_t[:, 0, 0:P]).then_inc(s("ckv_out"), 1)
                        nc.vector.tensor_copy(ckv_out[:, P:P + ROPE], ps_t[:, 1, 0:ROPE]).then_inc(s("ckv_out"), 1)
                        for m in range(4):
                            b = m % 2
                            dve.wait_ge(s("q_nope"), m + 1)
                            for j in (0, 1):
                                ins = nc.vector.tensor_copy(halves(q_h[0:NOPE, 2 * m + j, :]),
                                                            ps_s[b][NOPE * j:NOPE * j + NOPE, :, 0:NH2])
                            ins.then_inc(s("q_nope_read"), 1)
                        for m in (0, 1):
                            dve.wait_ge(s("q_rope"), m + 1)
                            for j in range(4):
                                rows = slice(ROPE * j, ROPE * j + ROPE)
                                link(nc.vector.tensor_copy(q_h[NOPE:QK, 4 * m + j, 0:NCTX], ps_s[0][rows, 0, 0:NCTX]))
                            pieces = ((0, NCTX, NH2), (1, 0, NH2))
                            at = 0
                            for bank, c0, c1_ in pieces:
                                w = c1_ - c0
                                link(nc.vector.tensor_tensor(t1[:, at:at + w], ps_s[0][:, bank, c0:c1_],
                                                             cos_t[:, at:at + w], ALU.mult))
                                link(nc.vector.tensor_tensor(t2[:, at:at + w], ps_s[1][:, bank, c0:c1_],
                                                             sin_t[:, at:at + w], ALU.mult))
                                at += w
                            for j in range(4):
                                rows = slice(ROPE * j, ROPE * j + ROPE)
                                ins = nc.vector.tensor_tensor(q_h[NOPE:QK, 4 * m + j, NCTX:N], t1[rows], t2[rows], ALU.add)
                                ins.then_inc(s("q_rope_read"), 1)
                        for m in range(4):
                            b = m % 2
                            dve.wait_ge(s("k_nope"), m + 1)
                            for j in (0, 1):
                                ins = nc.vector.tensor_copy(
                                    k_h[0:NOPE, 2 * m + j, :].rearrange("p (h n) -> p h n", h=2),
                                    ps_s[b][NOPE * j:NOPE * j + NOPE, :, 0:NALL // 2])
                            ins.then_inc(s("k_nope_read"), 1)
                        for kt in range(NALL // P):
                            dve.wait_ge(s("v_ps"), kt + 1)
                            nc.vector.tensor_copy(v_tok[:, kt, :], ps_o[kt % 2][:, :]).then_inc(s("v_read"), 1)

                        def maximum(u):
                            qt, h = units[u]
                            b = u % 2
                            dve.wait_ge(s("scores"), u + 1)
                            src = ps_s[b][:, 0, 0:P] if qt == 0 else ps_s[b][:, :, 0:NH2]
                            link(nc.vector.tensor_reduce(stat[b][:, 0:1], src, AX.X if qt == 0 else AX.XY, ALU.max))
                            nc.vector.tensor_scalar(stat[b][:, 1:2], stat[b][:, 0:1], -ATT_SCALE, None,
                                                    ALU.mult).then_inc(s("negmax"), 1)

                        def normalise(u):
                            qt, h = units[u]
                            b, nk = u % 2, len(keys(qt)) * P
                            dve.wait_ge(s("exp"), u + 1)
                            link(nc.vector.reciprocal(stat[b][:, 3:4], stat[b][:, 2:3]))
                            nc.vector.tensor_scalar(probs[b][:, 0:nk], probs[b][:, 0:nk], stat[b][:, 3:4], None,
                                                    ALU.mult).then_inc(s("probs"), 1)

                        def read_turned(u):
                            qt, h = units[u]
                            b, n = u % 2, len(keys(qt))
                            dve.wait_ge(s("turned"), u + 1)
                            if u >= 2:
                                dve.wait_ge(s("attended"), u - 1)
                            if n == 1:
                                nc.vector.tensor_copy(probs_t[b][:, 0:P], ps_t[:, 0, 0:P]).then_inc(s("probs_t"), 1)
                            else:
                                nc.vector.tensor_copy(probs_t[b][:, 0:384], ps_t[:, 0, 0:384]).then_inc(s("probs_ta"), 1)
                                nc.vector.tensor_copy(probs_t[b][:, 384:N], ps_t[:, 1, 0:256]).then_inc(s("probs_t"), 1)

                        def read_out(u):
                            qt, h = units[u]
                            b = u % 2
                            dve.wait_ge(s("attended"), u + 1)
                            rows = slice(VD * (h % 2), VD * (h % 2) + VD)
                            cs = slice(qt * P, qt * P + P)
                            nc.vector.tensor_copy(h_hi[rows, h // 2, cs], ps_o[b][rows, 0:P]).then_inc(s("att_hi"), 1)
                            dve.wait_ge(s("att_hi"), u + 1)
                            nc.vector.tensor_tensor(h_lo[rows, h // 2, cs], ps_o[b][rows, 0:P],
                                                    h_hi[rows, h // 2, cs].bitcast(F32), ALU.subtract
                                                    ).then_inc(s("att_read"), 1)
                        for u in range(len(units) + 2):
                            if u < len(units):
                                maximum(u)
                            if 1 <= u <= len(units):
                                normalise(u - 1)
                                read_turned(u - 1)
                            if u >= 2:
                                read_out(u - 2)

                    @block.tensor
                    def _(pe):
                        for name in ("inv_q", "inv_k", "w_uq", "w_ukv", "cache_ckv_t"):
                            pe.wait_ge(s("ld_" + name), 16)
                        pe.wait_ge(s("lat_sq"), 2)
                        for half in (0, 1):
                            cs = slice(half * NH2, half * NH2 + NH2)
                            nc.tensor.matmul(ps_s[0][:, half, 0:NH2], inv_q[:], sq[:, cs], start=True, stop=False)
                            last = nc.tensor.matmul(ps_s[0][:, half, 0:NH2], inv_q[:], sqb[:, cs], start=False, stop=True)
                        last.then_inc(s("cq_meansq"), 1)
                        pe.wait_ge(s("lat_sq"), 3)
                        for half in (0, 1):
                            cs = slice(half * NH2, half * NH2 + NH2)
                            last = nc.tensor.matmul(ps_s[1][:, half, 0:NH2], inv_k[:], sq[:, cs], start=True, stop=True)
                        last.then_inc(s("ckv_meansq"), 1)
                        pe.wait_ge(s("ckv_normed"), 1)
                        nc.tensor.transpose(ps_t[:, 0, 0:P], ckv[:, 0:NCTX], ident[:])
                        pe.wait_ge(s("kr_done"), 1)
                        nc.tensor.transpose(ps_t[:, 1, 0:ROPE], kr_new[:, 0:NCTX], ident[0:ROPE, 0:ROPE]
                                            ).then_inc(s("ctx_turned"), 1)

                        def q_product(ps, c0):
                            for half in (0, 1):
                                for k in (0, 1):
                                    ins = nc.tensor.matmul(ps[:, half, 0:NH2], w_uq[:, k, c0:c0 + P],
                                                           proj[:, M_CQ + k, half * NH2:half * NH2 + NH2],
                                                           start=(k == 0), stop=(k == 1))
                            return ins
                        pe.wait_ge(s("cq_normed"), 2)
                        for m in range(4):
                            if m >= 2:
                                pe.wait_ge(s("q_nope_read"), m - 1)
                            q_product(ps_s[m % 2], m * P).then_inc(s("q_nope"), 1)
                        pe.wait_ge(s("q_nope_read"), 4)
                        for m in (0, 1):
                            if m:
                                pe.wait_ge(s("q_rope_read"), 4 * m)
                            q_product(ps_s[0], 512 + m * P)
                            q_product(ps_s[1], 768 + m * P).then_inc(s("q_rope"), 1)
                        pe.wait_ge(s("q_rope_read"), 8)
                        for m in range(4):
                            if m >= 2:
                                pe.wait_ge(s("k_nope_read"), m - 1)
                            for half in (0, 1):
                                last = nc.tensor.matmul(ps_s[m % 2][:, half, 0:NALL // 2], w_ukv[:, 0, m * P:m * P + P],
                                                        ckv[:, half * (NALL // 2):(half + 1) * (NALL // 2)],
                                                        start=True, stop=True)
                            last.then_inc(s("k_nope"), 1)
                        for kt in range(NALL // P):
                            if kt >= 2:
                                pe.wait_ge(s("v_read"), kt - 1)
                            nc.tensor.matmul(ps_o[kt % 2][:, :], ckv[:, kt * P:kt * P + P], w_ukv[:, 1, :],
                                             start=True, stop=True).then_inc(s("v_ps"), 1)
                        pe.wait_ge(s("k_nope_read"), 4)
                        pe.wait_ge(s("v_read"), NALL // P)
                        pe.wait_ge(s("kh_rope"), 2 * HEADS)

                        def score(u):
                            qt, h = units[u]
                            if u >= 2:
                                pe.wait_ge(s("exp"), u - 1)
                            q = q_h[:, h, qt * P:qt * P + P]
                            if qt == 0:
                                last = nc.tensor.matmul(ps_s[u % 2][:, 0, 0:P], q, k_h[:, h, 0:P], start=True, stop=True)
                            else:
                                for half in (0, 1):
                                    c0 = P + half * NH2
                                    last = nc.tensor.matmul(ps_s[u % 2][:, half, 0:NH2], q, k_h[:, h, c0:c0 + NH2],
                                                            start=True, stop=True)
                            last.then_inc(s("scores"), 1)

                        def turn(u):
                            qt, h = units[u]
                            pe.wait_ge(s("probs"), u + 1)
                            if u:
                                pe.wait_ge(s("probs_t"), u)
                            for j in range(len(keys(qt))):
                                out = ps_t[:, j // 3, (j % 3) * P:(j % 3) * P + P]
                                last = nc.tensor.transpose(out, probs[u % 2][:, j * P:j * P + P], ident[:])
                            last.then_inc(s("turned"), 1)

                        def attend(u):
                            qt, h = units[u]
                            pe.wait_ge(s("probs_t"), u + 1)
                            if u >= 2:
                                pe.wait_ge(s("att_read"), u - 1)
                            kts = keys(qt)
                            r0 = VD * (h % 2)
                            for j, kt in enumerate(kts):
                                last = nc.tensor.matmul(ps_o[u % 2][r0:r0 + VD, 0:P], v_tok[:, kt, h * VD:h * VD + VD],
                                                        probs_t[u % 2][:, j * P:j * P + P],
                                                        start=(j == 0), stop=(j == len(kts) - 1))
                            last.then_inc(s("attended"), 1)
                        for u in range(len(units) + 2):
                            if u < len(units):
                                score(u)
                            if 1 <= u <= len(units):
                                turn(u - 1)
                            if u >= 2:
                                attend(u - 2)

                s.clear()

                with ExitStack() as c3:
                    W = NLAT + 384
                    rel = [sb(c3, f"rel{g}", [P, W]) for g in (0, 1)]
                    msk = [sb(c3, f"msk{g}", [P, W]) for g in (0, 1)]
                    dec = [sb(c3, f"dec{g}", [P, W]) for g in (0, 1)]
                    dmat = [sb(c3, f"dmat{h}", [P, W]) for h in range(RH)]
                    steps = sb(c3, "steps", [P, 2, NLAT])
                    ksteps = sb(c3, "ksteps", [P, 2 * RH])
                    state = sb(c3, "state", [P, 2, RH, DK])
                    inv_e = sb(c3, "inv_e", [P, P])
                    rv_tok = sb(c3, "rv_tok", [P, NT, 512])
                    rk_tok = sb(c3, "rk_tok", [P, 512])
                    kdec = sb(c3, "kdec", [P, 2, 512])
                    lgw = sb(c3, "lgw", [P, 8, 8])
                    scm = [sb(c3, f"scm{b}", [P, NLAT]) for b in (0, 1)]
                    qdec = [sb(c3, f"qdec{g}", [P, NLAT]) for g in (0, 1)]
                    st_out = sb(c3, "st_out", [P, 2, RH, DK])
                    y_t = act_buf
                    var, root, r, t = (act_buf[:, k, :] for k in (4, 5, 6, 7))
                    ps_sc = [pb(c3, f"ps_sc{b}", [P, 512]) for b in (0, 1)]
                    ps_y = [pb(c3, f"ps_y{b}", [P, 512]) for b in (0, 1)]
                    ps_n = pb(c3, "ps_n3", [P, 2, 512])
                    units = [(h, j) for h in range(RH) for j in range(NT)]
                    lg = lgw[:, 7, :]
                    block = c3.enter_context(nc.Block())

                    @block.sync
                    def _(sp):
                        for dst, name in ((rel[0][:], "rel0"), (rel[1][:], "rel1"), (msk[0][:], "msk0"),
                                          (msk[1][:], "msk1"), (steps[:], "steps"), (ksteps[:], "ksteps"),
                                          (state[:], "state"), (inv_e[:], "inv_k")):
                            sp.dma_start(dst, a[name]).then_inc(s("ret_ld"), 16)
                        sp.wait_ge(s("st_read"), 2 * RH)
                        for g, dst in ((0, new_sf), (1, new_sb)):
                            sp.dma_start(dst, st_out[:, g, :, :]).then_inc(s("st_state"), 16)
                        sp.wait_ge(s("st_state"), 32)

                    @block.scalar
                    def _(act):
                        act.wait_ge(s("lg_abs"), 1)
                        nc.scalar.activation(lgw[:, 1, :], lgw[:, 0, :], ACT.Exp, scale=-1.0).then_inc(s("lg_exp"), 1)
                        act.wait_ge(s("lg_done"), 1)
                        act.wait_ge(s("ret_ld"), 16 * 8)
                        act.wait_ge(s("kst_mul"), 1)
                        nc.scalar.activation(ksteps[:], ksteps[:], ACT.Exp).then_inc(s("kst_exp"), 1)
                        for h in range(RH):
                            for g in (0, 1):
                                if h:
                                    act.wait_ge(s("dmat"), h)
                                nc.scalar.activation(dec[g][:], rel[g][:], ACT.Exp, scale=lg[:, RH * g + h:RH * g + h + 1]
                                                     ).then_inc(s("dec"), 1)
                        for h in range(RH):
                            for g in (0, 1):
                                if h:
                                    act.wait_ge(s("ret_av"), NT * h)
                                nc.scalar.activation(qdec[g][:], steps[:, g, :], ACT.Exp,
                                                     scale=lg[:, RH * g + h:RH * g + h + 1]).then_inc(s("qexp"), 1)
                        for h in range(RH):
                            act.wait_ge(s("centred"), h + 1)
                            if h:
                                act.wait_ge(s("gn_normed"), h)
                            nc.scalar.activation(t, y_t[:, h, :], ACT.Square).then_inc(s("gn_sq"), 1)
                            act.wait_ge(s(f"gn{h}_var"), 1)
                            nc.scalar.activation(root, var, ACT.Sqrt).then_inc(s(f"gn{h}_root"), 1)
                            nc.scalar.activation(proj[:, M_RG + h, :], proj[:, M_RG + h, :], ACT.Silu).then_inc(s("silu_g"), 1)
                            act.wait_ge(s("ret_out"), h + 1)
                            nc.scalar.activation(h_hi[:, RH + h, :], y_t[:, h, :], ACT.Copy).then_inc(s("ret_hi"), 1)

                    @block.vector
                    def _(dve):
                        link = Chain(dve, s("dve3"))
                        V = nc.vector
                        x = cols[:, C_LOG:C_LOG + 8]
                        link(V.tensor_scalar(lgw[:, 0, :], x, -1.0, None, ALU.mult))
                        V.tensor_tensor(lgw[:, 0, :], lgw[:, 0, :], x, ALU.max).then_inc(s("lg_abs"), 1)
                        dve.wait_ge(s("lg_exp"), 1)
                        link(V.tensor_scalar(lgw[:, 2, :], lgw[:, 1, :], 2.0, None, ALU.add))
                        link(V.reciprocal(lgw[:, 3, :], lgw[:, 2, :]))
                        link(V.tensor_tensor(lgw[:, 4, :], lgw[:, 1, :], lgw[:, 3, :], ALU.mult))
                        link(V.tensor_tensor(lgw[:, 5, :], lgw[:, 4, :], lgw[:, 4, :], ALU.mult))
                        link(V.tensor_scalar(lgw[:, 6, :], lgw[:, 5, :], 1 / 19, 1 / 17, ALU.mult, ALU.add))
                        for n in range(15, 0, -2):
                            link(V.tensor_tensor(lgw[:, 6, :], lgw[:, 6, :], lgw[:, 5, :], ALU.mult))
                            link(V.tensor_scalar(lgw[:, 6, :], lgw[:, 6, :], 1 / n, None, ALU.add))
                        link(V.tensor_tensor(lgw[:, 6, :], lgw[:, 6, :], lgw[:, 4, :], ALU.mult))
                        link(V.tensor_scalar(lgw[:, 0, :], x, 0.0, None, ALU.min))
                        V.scalar_tensor_tensor(out=lg, in0=lgw[:, 6, :], scalar=-2.0, in1=lgw[:, 0, :],
                                               op0=ALU.mult, op1=ALU.add).then_inc(s("lg_done"), 1)
                        dve.wait_ge(s("lg_done"), 1)
                        dve.wait_ge(s("ret_ld"), 16 * 8)
                        V.tensor_tensor(ksteps[:], ksteps[:], lg, ALU.mult).then_inc(s("kst_mul"), 1)
                        for k in range(NT + 1):
                            dve.wait_ge(s("turned3"), k + 1)
                            dst = rv_tok[:, k, :] if k < NT else rk_tok[:, :]
                            V.tensor_copy(dst, ps_sc[k % 2][:, :]).then_inc(s("turned3_read"), 1)
                        dve.wait_ge(s("turned3_read"), NT + 1)
                        dve.wait_ge(s("kst_exp"), 1)
                        for g in (0, 1):
                            for h in range(RH):
                                cs = slice(h * DK, h * DK + DK)
                                V.tensor_scalar(kdec[:, g, cs], rk_tok[:, cs], ksteps[:, RH * g + h:RH * g + h + 1],
                                                RET_SCALE, ALU.mult, ALU.mult).then_inc(s("kdec"), 1)
                        for g in (0, 1):
                            for h in range(RH):
                                k = g * RH + h
                                dve.wait_ge(s("st_mm"), k + 1)
                                V.tensor_copy(st_out[:, g, h, :], ps_y[k % 2][:, 0:DK]).then_inc(s("st_read"), 1)
                        for h in range(RH):
                            dve.wait_ge(s("dec"), 2 * h + 2)
                            link(V.tensor_tensor(dec[0][:], dec[0][:], msk[0][:], ALU.mult))
                            link(V.tensor_tensor(dec[1][:], dec[1][:], msk[1][:], ALU.mult))
                            V.tensor_tensor(dmat[h][:], dec[0][:], dec[1][:], ALU.add).then_inc(s("dmat"), 1)
                        dve.wait_ge(s("dmat"), RH)
                        for u, (h, j) in enumerate(units):
                            if j == 0:
                                dve.wait_ge(s("qexp"), 2 * h + 2)
                                for g in (0, 1):
                                    V.tensor_tensor(qdec[g][:], qdec[g][:], proj[:, M_RQ + h, NCTX:N], ALU.mult
                                                    ).then_inc(s("qdec"), 1)
                            dve.wait_ge(s("ret_sc"), u + 1)
                            if u >= 2:
                                dve.wait_ge(s("ret_av"), u - 1)
                            n, c0 = (NCTX, 384) if j == 0 else (NLAT, 384 - P * (j - 1))
                            V.scalar_tensor_tensor(out=scm[u % 2][:, 0:n], in0=ps_sc[u % 2][:, 0:n], scalar=RET_SCALE,
                                                   in1=dmat[h][:, c0:c0 + n], op0=ALU.mult, op1=ALU.mult
                                                   ).then_inc(s("ret_masked"), 1)
                            if j == 1:
                                dve.wait_ge(s("ret_av"), 5 * h + 1)
                                V.tensor_copy(y_t[:, h, 0:NCTX], ps_y[0][:, 0:NCTX]).then_inc(s("y_ctx"), 1)
                            if j == NT - 1:
                                dve.wait_ge(s("ret_av"), NT * h + NT)
                                V.tensor_copy(y_t[:, h, NCTX:N], ps_y[1][:, :]).then_inc(s("y_lat"), 1)
                        dve.wait_ge(s("y_lat"), RH)
                        for h in range(RH):
                            dve.wait_ge(s("gn_mean"), h + 1)
                            V.tensor_tensor(halves(y_t[:, h, :]), halves(y_t[:, h, :]), ps_n[:, :, 0:NH2], ALU.subtract
                                            ).then_inc(s("centred"), 1)
                            dve.wait_ge(s("gn_var"), h + 1)
                            rstd_ops(dve, link, f"gn{h}", ps_n[:, :, 0:NH2], halves(var), var, root, r, t)
                            V.scalar_tensor_tensor(out=y_t[:, h, :], in0=y_t[:, h, :], scalar=cols[:, C_GN + h:C_GN + h + 1],
                                                   in1=r, op0=ALU.mult, op1=ALU.mult).then_inc(s("gn_normed"), 1)
                            dve.wait_ge(s("gn_normed"), h + 1)
                            dve.wait_ge(s("silu_g"), h + 1)
                            V.tensor_tensor(y_t[:, h, :], y_t[:, h, :], proj[:, M_RG + h, :], ALU.mult
                                            ).then_inc(s("ret_out"), 1)
                            dve.wait_ge(s("ret_hi"), h + 1)
                            V.tensor_tensor(h_lo[:, RH + h, :], y_t[:, h, :], h_hi[:, RH + h, :].bitcast(F32), ALU.subtract
                                            ).then_inc(s("ret_lo"), 1)

                    @block.tensor
                    def _(pe):
                        pe.wait_ge(s("ret_ld"), 16 * 8)
                        for k in range(NT + 1):
                            if k >= 2:
                                pe.wait_ge(s("turned3_read"), k - 1)
                            for h in range(RH):
                                src = proj[:, M_RV + h, k * P:k * P + P] if k < NT else proj[:, M_RK + h, 0:P]
                                last = nc.tensor.transpose(ps_sc[k % 2][:, h * P:h * P + P], src, ident[:])
                            last.then_inc(s("turned3"), 1)
                        pe.wait_ge(s("turned3_read"), NT + 1)
                        pe.wait_ge(s("kdec"), 2 * RH)
                        for k in range(2 * RH):
                            g, h = k // RH, k % RH
                            cs = slice(h * DK, h * DK + DK)
                            if k >= 2:
                                pe.wait_ge(s("st_read"), k - 1)
                            nc.tensor.matmul(ps_y[k % 2][:, 0:DK], kdec[:, g, cs], rv_tok[:, 0, cs], start=True, stop=True
                                             ).then_inc(s("st_mm"), 1)
                        pe.wait_ge(s("st_read"), 2 * RH)

                        def score(u):
                            h, j = units[u]
                            if u >= 2:
                                pe.wait_ge(s("ret_masked"), u - 1)
                            qs = slice(0, NCTX) if j == 0 else slice(NCTX, N)
                            nc.tensor.matmul(ps_sc[u % 2][:, 0:qs.stop - qs.start], proj[:, M_RK + h, j * P:j * P + P],
                                             proj[:, M_RQ + h, qs], start=True, stop=True).then_inc(s("ret_sc"), 1)

                        def values(u):
                            h, j = units[u]
                            pe.wait_ge(s("ret_masked"), u + 1)
                            v = rv_tok[:, j, h * DK:h * DK + DK]
                            if j == 0:
                                if h:
                                    pe.wait_ge(s("y_ctx"), h)
                                nc.tensor.matmul(ps_y[0][:, 0:NCTX], v, scm[u % 2][:, 0:NCTX], start=True, stop=True
                                                 ).then_inc(s("ret_av"), 1)
                                return
                            if j == 1:
                                if h:
                                    pe.wait_ge(s("y_lat"), h)
                                pe.wait_ge(s("qdec"), 2 * h + 2)
                                for g in (0, 1):
                                    nc.tensor.matmul(ps_y[1][:, :], state[:, g, h, :], qdec[g][:], start=(g == 0), stop=False)
                            last = nc.tensor.matmul(ps_y[1][:, :], v, scm[u % 2][:, :], start=False, stop=(j == NT - 1))
                            last.then_inc(s("ret_av"), 1)
                        for u in range(len(units) + 1):
                            if u < len(units):
                                score(u)
                            if u:
                                values(u - 1)
                        pe.wait_ge(s("y_lat"), RH)
                        pe.wait_ge(s("y_ctx"), RH)
                        for h in range(RH):
                            if h:
                                pe.wait_ge(s(f"gn{h - 1}_var"), 1)
                            for half in (0, 1):
                                last = nc.tensor.matmul(ps_n[:, half, 0:NH2], inv_e[:], y_t[:, h, half * NH2:half * NH2 + NH2],
                                                        start=True, stop=True)
                            last.then_inc(s("gn_mean"), 1)
                            pe.wait_ge(s("gn_sq"), h + 1)
                            for half in (0, 1):
                                last = nc.tensor.matmul(ps_n[:, half, 0:NH2], inv_e[:], t[:, half * NH2:half * NH2 + NH2],
                                                        start=True, stop=True)
                            last.then_inc(s("gn_var"), 1)

            s.clear()

            with ExitStack() as c4:
                banks = [pb(c4, f"mrg_ps{b}", [P, 4, 512]) for b in (0, 1)]
                with ExitStack() as c:
                    gbuf = [[sb(c, f"gbuf{g}{b}", [P, N]) for b in (0, 1)] for g in (0, 1)]
                    prt = [sb(c, f"prt{b}", [P, N]) for b in (0, 1)]
                    lin = Linear(c, "mrg", a["w_up"], KC, banks)
                    block = c.enter_context(nc.Block())

                    @block.sync
                    def _(sp):
                        def step(i):
                            for b in (0, 1):
                                lin.load(sp, i, b)
                                sp.wait_ge(lin.sem("evac", b), i)
                                for g in (0, 1):
                                    sp.dma_start(gbuf[g][b][:], gates_d[bass.ds(2 * i + b + KC * g, 1)].rearrange("o p m -> p (o m)")
                                                 ).then_inc(s(f"gate_ld{b}{g}"), 16)
                        run(sp, 0, KC // 2, step)

                    @block.scalar
                    def _(act):
                        def step(i):
                            for b in (0, 1):
                                lin.head(act, i, b)
                        run(act, 0, KC // 2, step)

                    @block.gpsimd
                    def _(pool):
                        def step(i):
                            for b in (0, 1):
                                lin.rest(pool, i, b)
                        run(pool, 0, KC // 2, step)

                    @block.vector
                    def _(dve):
                        def step(i):
                            for b in (0, 1):
                                lin.wait_out(dve, i, b)
                                for g in (0, 1):
                                    dve.wait_ge(s(f"gate_ld{b}{g}"), 16 * i + 16)
                                nc.vector.tensor_tensor(halves(prt[b][:, :]), lin.out(b, 0), halves(gbuf[0][b][:, :]), ALU.mult
                                                        ).then_inc(s(f"prt_a{b}"), 1)
                                nc.vector.tensor_tensor(halves(gbuf[1][b][:, :]), lin.out(b, 1), halves(gbuf[1][b][:, :]), ALU.mult
                                                        ).then_inc(s(f"prt_b{b}"), 1)
                                dve.wait_ge(s(f"prt_a{b}"), i + 1)
                                dve.wait_ge(s(f"prt_b{b}"), i + 1)
                                nc.vector.tensor_tensor(act_buf[:, bass.ds(2 * i + b, 1), :].rearrange("p o n -> p (o n)"),
                                                        prt[b][:, :], gbuf[1][b][:, :], ALU.add).then_inc(lin.sem("evac", b), 1)
                        run(dve, 0, KC // 2, step)

                    @block.tensor
                    def _(pe):
                        def step(i):
                            for b in (0, 1):
                                lin.product(pe, i, b, ((0, 4), (4, 8)))
                        run(pe, 0, KC // 2, step)

                def split_act(act, tag):
                    for kc in range(KC):
                        nc.scalar.activation(h_hi[:, kc, :], act_buf[:, kc, :], ACT.Copy).then_inc(s(tag + "_hi"), 1)

                def split_dve(dve, tag):
                    for kc in range(KC):
                        dve.wait_ge(s(tag + "_hi"), kc + 1)
                        nc.vector.tensor_tensor(h_lo[:, kc, :], act_buf[:, kc, :], h_hi[:, kc, :].bitcast(F32),
                                                ALU.subtract).then_inc(s(tag + "_split"), 1)

                with ExitStack() as c:
                    lin = Linear(c, "wo", a["w_o"], KC, banks)
                    inv_d = sb(c, "inv_d4", [P, P])
                    wrk = [sb(c, f"n2_{n}", [P, N]) for n in ("var", "root", "r", "t")]
                    x2_tok = [sb(c, f"x2_tok{b}", [P, D]) for b in (0, 1)]
                    block = c.enter_context(nc.Block())

                    @block.sync
                    def _(sp):
                        sp.dma_start(inv_d[:], a["inv_d"]).then_inc(s("ld_inv4"), 16)
                        def step(i):
                            for b in (0, 1):
                                lin.load(sp, i, b)
                        run(sp, 0, KC // 2, step)
                        for tt in range(NT):
                            sp.wait_ge(s("x2_read"), 2 * tt + 2)
                            sp.dma_start(x2_d[tt], x2_tok[tt % 2][:]).then_inc(s(f"x2_st{tt % 2}"), 16)
                        sp.wait_ge(s("x2_st0"), 48)
                        sp.wait_ge(s("x2_st1"), 32)

                    @block.scalar
                    def _(act):
                        split_act(act, "m")
                        def step(i):
                            for b in (0, 1):
                                lin.head(act, i, b)
                        run(act, 0, KC // 2, step)
                        for b in (0, 1):
                            act.wait_ge(lin.sem("evac", b), KC // 2)
                        for kc in range(KC):
                            nc.scalar.activation(act_buf[:, kc, :], x_t[:, kc, :], ACT.Square).then_inc(s("n2_sq"), 1)
                        norm_act(act, "n2", wrk)

                    @block.gpsimd
                    def _(pool):
                        def step(i):
                            for b in (0, 1):
                                lin.rest(pool, i, b)
                        run(pool, 0, KC // 2, step)

                    @block.vector
                    def _(dve):
                        link = Chain(dve, s("dve4"))
                        split_dve(dve, "m")
                        def step(i):
                            for b in (0, 1):
                                lin.wait_out(dve, i, b)
                                m = 2 * i + b
                                xm = x_t[:, bass.ds(m, 1), :].rearrange("p o n -> p (o n)")
                                gm = [mod[:, bass.ds(m + 2 * KC, 1), g] for g in (0, 1)]
                                ps = lin.ps[b]
                                for g, bank, c0, c1_, x0 in ((0, 0, 0, NCTX, 0), (1, 0, NCTX, NH2, NCTX), (1, 1, 0, NH2, NH2)):
                                    ins = nc.vector.scalar_tensor_tensor(
                                        out=xm[:, x0:x0 + c1_ - c0], in0=ps[:, bank, c0:c1_], scalar=gm[g],
                                        in1=xm[:, x0:x0 + c1_ - c0], op0=ALU.mult, op1=ALU.add)
                                ins.then_inc(lin.sem("evac", b), 1)
                        run(dve, 0, KC // 2, step)
                        norm_dve(dve, link, "n2", banks[0][:, 0:2, :], wrk, C_FFN, 3 * KC, 4 * KC)
                        for k in range(2 * NT):
                            if k >= 4:
                                dve.wait_ge(s(f"x2_st{(k // 2) % 2}"), 16 * (k // 4))
                            dve.wait_ge(s("x2_turned"), k + 1)
                            nc.vector.tensor_copy(x2_tok[(k // 2) % 2][:, 512 * (k % 2):512 * (k % 2) + 512],
                                                  banks[1][:, k % 4, :]).then_inc(s("x2_read"), 1)

                    @block.tensor
                    def _(pe):
                        pe.wait_ge(s("m_split"), KC)
                        def step(i):
                            for b in (0, 1):
                                lin.product(pe, i, b)
                        run(pe, 0, KC // 2, step)
                        for b in (0, 1):
                            pe.wait_ge(lin.sem("evac", b), KC // 2)
                        pe.wait_ge(s("ld_inv4"), 16)
                        norm_pe(pe, "n2", act_buf, inv_d, banks[0], "n2_sq")
                        for k in range(2 * NT):
                            if k >= 4:
                                pe.wait_ge(s("x2_read"), k - 3)
                            for j in range(4):
                                last = nc.tensor.transpose(banks[1][:, k % 4, j * P:j * P + P],
                                                           x_t[:, 4 * (k % 2) + j, (k // 2) * P:(k // 2) * P + P], ident[:])
                            last.then_inc(s("x2_turned"), 1)

                with ExitStack() as c:
                    lin = Linear(c, "wq", a["w_q"], 16, banks)
                    q_t = sb(c, "q_t", [P, 16, N])
                    keys_t = sb(c, "keys_t", [P, 16, NK])
                    sc_tok = [sb(c, f"sc_tok{b}", [P, 16 * NK]) for b in (0, 1)]
                    block = c.enter_context(nc.Block())

                    @block.sync
                    def _(sp):
                        sp.dma_start(keys_t[:], a["keys_t"]).then_inc(s("ld_keys"), 16)
                        def step(i):
                            for b in (0, 1):
                                lin.load(sp, i, b)
                        run(sp, 0, 8, step)
                        for tt in range(NT):
                            sp.wait_ge(s("sc_read"), 4 * tt + 4)
                            sp.dma_start(scores_d[tt], sc_tok[tt % 2][:]).then_inc(s(f"sc_st{tt % 2}"), 16)
                        sp.wait_ge(s("sc_st0"), 48)
                        sp.wait_ge(s("sc_st1"), 32)

                    @block.scalar
                    def _(act):
                        def step(i):
                            for b in (0, 1):
                                lin.head(act, i, b)
                        run(act, 0, 8, step)

                    @block.gpsimd
                    def _(pool):
                        def step(i):
                            for b in (0, 1):
                                lin.rest(pool, i, b)
                        run(pool, 0, 8, step)

                    @block.vector
                    def _(dve):
                        def step(i):
                            for b in (0, 1):
                                lin.wait_out(dve, i, b)
                                nc.vector.tensor_copy(
                                    q_t[:, bass.ds(2 * i + b, 1), :].rearrange("p o (h n) -> p (o h) n", h=2),
                                    lin.out(b)).then_inc(lin.sem("evac", b), 1)
                        run(dve, 0, 8, step)
                        for k in range(4 * NT):
                            if k >= 8:
                                dve.wait_ge(s(f"sc_st{(k // 4) % 2}"), 16 * (k // 8))
                            dve.wait_ge(s("sc_mm"), k + 1)
                            nc.vector.tensor_copy(sc_tok[(k // 4) % 2][:, 512 * (k % 4):512 * (k % 4) + 512],
                                                  banks[0][:, k % 4, :]).then_inc(s("sc_read"), 1)

                    @block.tensor
                    def _(pe):
                        def step(i):
                            for b in (0, 1):
                                lin.product(pe, i, b)
                        run(pe, 0, 8, step)
                        for b in (0, 1):
                            pe.wait_ge(lin.sem("evac", b), 8)
                        pe.wait_ge(s("ld_keys"), 16)
                        for k in range(4 * NT):
                            if k >= 4:
                                pe.wait_ge(s("sc_read"), k - 3)
                            for j in range(4):
                                m = 4 * (k % 4) + j
                                last = nc.tensor.matmul(banks[0][:, k % 4, j * NK:j * NK + NK],
                                                        q_t[:, m, (k // 4) * P:(k // 4) * P + P], keys_t[:, m, :],
                                                        start=True, stop=True)
                            last.then_inc(s("sc_mm"), 1)

        s.clear()

        with ExitStack() as c5:
            NBATCH = P // OB
            PLAIN, LEAD = 4, 8
            SEG = PLAIN + NBATCH
            TAIL = NK - LEAD - NT * SEG
            QB = OB // 2
            sc = sb(c5, "sc", [P, 16, NK])
            sc2 = sb(c5, "sc2", [P, NK])
            val = sb(c5, "val", [P, 16, TOPK])
            idx = sb(c5, "idx", [P, 16, TOPK], U32)
            idxf = sb(c5, "idxf", [P, 16, TOPK])
            cand = sb(c5, "cand", [P, TOPK * TOPK])
            cand2 = sb(c5, "cand2", [P, TOPK * TOPK])
            cval = sb(c5, "cval", [P, PH, TOPK])
            cidx = sb(c5, "cidx", [P, PH, TOPK], U32)
            part = sb(c5, "part", [P, 2, PICKS], U32)
            partf = sb(c5, "partf", [P, 2, PICKS])
            eq = sb(c5, "eq", [P, PICKS, TOPK])
            pick = sb(c5, "pick", [P, 3, PICKS])
            red = sb(c5, "red", [P, 2, PH])
            hold = sb(c5, "hold", [P, 1])
            pick_t = sb(c5, "pick_t", [P, 3, P])
            iota_r = sb(c5, "iota_r", [P, NK])
            o1 = [sb(c5, f"o1_{b}", [P, OB, NK]) for b in (0, 1)]
            o2 = [sb(c5, f"o2_{b}", [P, OB, NK]) for b in (0, 1)]
            stage = [sb(c5, f"stage{b}", [P, NK, WB]) for b in (0, 1)]
            ga = [sb(c5, f"ga{b}", [P, N]) for b in (0, 1)]
            banks = [pb(c5, f"u_ps{b}", [P, 2, 512]) for b in (0, 1)]
            ps_p = pb(c5, "ps_p", [P, 3, P])
            ps_w = [pb(c5, f"ps_w{b}", [P, QB, NK]) for b in (0, 1)]
            lin = Linear(c5, "u", a["u"], NK, banks)
            ROUTE_OPS = 16 * 5 + PH * 6

            def first_pair(t):
                return LEAD // 2 + (SEG // 2) * t
            block = c5.enter_context(nc.Block())

            @block.sync
            def _(sp):
                sp.dma_start(iota_r[:], a["iota_r"]).then_inc(s("ld_iota"), 16)
                sp.dma_start(sc[:, :, :].rearrange("p m k -> p (m k)"), scores_d[0]).then_inc(s("ld_sc"), 16)

                def pairs(i):
                    for b in (0, 1):
                        lin.load(sp, i, b)
                run(sp, 0, LEAD // 2, pairs)

                def tile(t, more):
                    for m in range(SEG):
                        lin.load(sp, first_pair(t) + m // 2, m % 2)
                        if m == PLAIN - 1 and more:
                            sp.wait_ge(s("routed"), ROUTE_OPS * (t + 1))
                            sp.dma_start(sc[:, :, :].rearrange("p m k -> p (m k)"),
                                         scores_d[bass.ds(t + 1, 1)].rearrange("o p m -> p (o m)")
                                         ).then_inc(s("ld_sc"), 16)
                run(sp, 0, NT - 1, lambda t: tile(t, True))
                tile(NT - 1, False)
                run(sp, (NK - TAIL) // 2, NK // 2, pairs)
                for b in (0, 1):
                    sp.wait_ge(s(f"wgt_st{b}"), 16 * NT)
                    sp.wait_ge(s(f"act_st{b}"), 16 * (NK // 2))

            @block.scalar
            def _(act):
                def column(pair, m, ahead=True):
                    b = m % 2
                    if ahead:
                        lin.head(act, pair + m, 1 - b)
                    lin.wait_out(act, pair, b)
                    act.wait_ge(s(f"act_st{b}"), 16 * pair)
                    nc.scalar.activation(halves(ga[b][:, :]), lin.out(b), ACT.Gelu_apprx_tanh
                                         ).then_inc(lin.sem("evac", b), 1)
                    act.wait_ge(lin.sem("evac", b), pair + 1)
                    act.dma_start(act_d[bass.ds(2 * pair + b, 1)].rearrange("o p m -> p (o m)"), ga[b][:]
                                  ).then_inc(s(f"act_st{b}"), 16)

                def pairs(i):
                    for m in (0, 1):
                        column(i, m)
                lin.head(act, 0, 0)
                run(act, 0, LEAD // 2, pairs)

                def tile(t):
                    for m in range(SEG):
                        k = m - PLAIN
                        if m == 1:
                            act.wait_ge(s("softmax_in"), t + 1)
                            nc.scalar.activation(pick[:, 2, :], pick[:, 2, :], ACT.Exp).then_inc(s("softmax_exp"), 1)
                        column(first_pair(t) + m // 2, m % 2)
                        if k < 0:
                            continue
                        blk = k // (NBATCH // 2)
                        if k % (NBATCH // 2) == 0:
                            act.wait_ge(s(f"wgt_st{blk}"), 16 * t)
                        for half in (0, 1):
                            n0 = (k % (NBATCH // 2)) * OB + half * QB
                            act.wait_ge(s(f"gates_mm{half}"), NBATCH * t + k + 1)
                            nc.scalar.activation(stage[blk][:, :, n0:n0 + QB],
                                                 ps_w[half][:, :, :].rearrange("p n k -> p k n"), ACT.Copy
                                                 ).then_inc(s(f"gates_read{half}"), 1)
                        if k % (NBATCH // 2) == NBATCH // 2 - 1:
                            act.wait_ge(s("gates_read0"), NBATCH * t + k + 1)
                            act.wait_ge(s("gates_read1"), NBATCH * t + k + 1)
                            act.dma_start(wgt_d[:, bass.ds(2 * t + blk, 1), :].rearrange("p o m -> p (o m)"),
                                          stage[blk][:, :, :].rearrange("p k n -> p (k n)")
                                          ).then_inc(s(f"wgt_st{blk}"), 16)
                run(act, 0, NT, tile)
                run(act, (NK - TAIL) // 2, NK // 2 - 1, pairs)
                column(NK // 2 - 1, 0)
                column(NK // 2 - 1, 1, ahead=False)

            @block.gpsimd
            def _(pool):
                def pairs(i):
                    for b in (0, 1):
                        lin.rest(pool, i, b)
                run(pool, 0, NK // 2, pairs)

            @block.vector
            def _(dve):
                V = nc.vector
                dve.wait_ge(s("ld_iota"), 16)

                def route(t, m, n):
                    def counted(ins):
                        nonlocal n
                        n += 1
                        ins.then_inc(s("routed"), 1)

                    def settle():
                        dve.wait_ge(s("routed"), ROUTE_OPS * t + n)

                    def held():
                        settle()
                        V.memset(hold[:], 0.0)
                    if m == 0:
                        dve.wait_ge(s("ld_sc"), 16 * t + 16)
                        V.memset(hold[:], 0.0)
                    counted(V.max(val[:, m, 0:8], sc[:, m, :]))
                    held()
                    counted(V.match_replace(sc2[:], val[:, m, 0:8], sc[:, m, :], LOW))
                    counted(V.max_index(idx[:, m, 0:8], val[:, m, 0:8], sc[:, m, :]))
                    held()
                    counted(V.max(val[:, m, 8:16], sc2[:]))
                    held()
                    counted(V.max_index(idx[:, m, 8:16], val[:, m, 8:16], sc2[:]))
                    if m % 2 == 0:
                        return n
                    h = m // 2
                    settle()
                    counted(V.tensor_tensor(cand[:, :].rearrange("p (a b) -> p a b", a=TOPK),
                                            val[:, 2 * h, :].unsqueeze(2).to_broadcast([P, TOPK, TOPK]),
                                            val[:, 2 * h + 1, :].unsqueeze(1).to_broadcast([P, TOPK, TOPK]), ALU.add))
                    held()
                    counted(V.max(cval[:, h, 0:8], cand[:]))
                    held()
                    counted(V.match_replace(cand2[:], cval[:, h, 0:8], cand[:], LOW))
                    counted(V.max_index(cidx[:, h, 0:8], cval[:, h, 0:8], cand[:]))
                    held()
                    counted(V.max(cval[:, h, 8:16], cand2[:]))
                    held()
                    counted(V.max_index(cidx[:, h, 8:16], cval[:, h, 8:16], cand2[:]))
                    return n

                def decide(t):
                    dve.wait_ge(s("routed"), ROUTE_OPS * t + ROUTE_OPS)
                    V.tensor_tensor(pick[:, 2, :].rearrange("p (h j) -> p h j", h=PH), cval[:, :, :],
                                    cval[:, :, 0:1].to_broadcast([P, PH, TOPK]), ALU.subtract
                                    ).then_inc(s("softmax_in"), 1)
                    flat = cidx[:, :, :].rearrange("p h j -> p (h j)")
                    V.tensor_scalar(part[:, 0, :], flat, 4, None, ALU.logical_shift_right).then_inc(s("part"), 1)
                    V.tensor_scalar(part[:, 1, :], flat, 15, None, ALU.bitwise_and).then_inc(s("part"), 1)
                    V.tensor_copy(idxf[:], idx[:]).then_inc(s("part"), 1)
                    dve.wait_ge(s("part"), 3 * t + 3)
                    V.tensor_copy(partf[:], part[:]).then_inc(s("partf"), 1)
                    dve.wait_ge(s("partf"), t + 1)
                    side = idxf[:, :, :].rearrange("p (h s) a -> p s h a", s=2)
                    for g in (0, 1):
                        V.tensor_tensor(eq[:], iota_r[:, 0:TOPK].unsqueeze(1).to_broadcast([P, PICKS, TOPK]),
                                        partf[:, g, :].unsqueeze(2).to_broadcast([P, PICKS, TOPK]),
                                        ALU.is_equal).then_inc(s("eq"), 1)
                        dve.wait_ge(s("eq"), 2 * t + g + 1)
                        V.tensor_tensor(eq[:, :, :].rearrange("p (h j) a -> p h j a", h=PH),
                                        eq[:, :, :].rearrange("p (h j) a -> p h j a", h=PH),
                                        side[:, g].unsqueeze(2).to_broadcast([P, PH, TOPK, TOPK]),
                                        ALU.mult).then_inc(s("eqk"), 1)
                        dve.wait_ge(s("eqk"), 2 * t + g + 1)
                        V.tensor_reduce(pick[:, g, :], eq[:], AX.X, ALU.add).then_inc(s("picked"), 1)
                        dve.wait_ge(s("picked"), 2 * t + g + 1)
                    gates = pick[:, 2, :].rearrange("p (h j) -> p h j", h=PH)
                    dve.wait_ge(s("softmax_exp"), t + 1)
                    V.tensor_reduce(red[:, 0, :], gates, AX.X, ALU.add).then_inc(s("sum"), 1)
                    dve.wait_ge(s("sum"), t + 1)
                    V.reciprocal(red[:, 1, :], red[:, 0, :]).then_inc(s("inv_sum"), 1)
                    dve.wait_ge(s("inv_sum"), t + 1)
                    V.tensor_tensor(gates, gates, red[:, 1, :].unsqueeze(2).to_broadcast([P, PH, TOPK]), ALU.mult
                                    ).then_inc(s("gated"), 1)
                    dve.wait_ge(s("picks_turned"), t + 1)
                    V.tensor_copy(pick_t[:], ps_p[:]).then_inc(s("pick_t"), 1)
                    dve.wait_ge(s("pick_t"), t + 1)

                def onehots(t, k):
                    iota8 = iota_r[:, :].unsqueeze(1).to_broadcast([P, OB, NK])
                    b, cs = k % 2, slice(k * OB, k * OB + OB)

                    def spread(n):
                        return pick_t[:, n, cs].unsqueeze(2).to_broadcast([P, OB, NK])
                    dve.wait_ge(s("gates_mm1"), NBATCH * t + max(k - 1, 0))
                    V.tensor_tensor(o1[b][:], iota8, spread(0), ALU.is_equal).then_inc(s("oh1"), 1)
                    V.tensor_tensor(o2[b][:], iota8, spread(1), ALU.is_equal).then_inc(s("oh2"), 1)
                    dve.wait_ge(s("oh2"), NBATCH * t + k + 1)
                    V.tensor_tensor(o2[b][:], o2[b][:], spread(2), ALU.mult).then_inc(s("onehot"), 1)

                def tile(t, more):
                    decide(t)
                    n = 0
                    for k in range(NBATCH):
                        onehots(t, k)
                        if more:
                            n = route(t + 1, k, n)
                n = 0
                for m in range(16):
                    n = route(0, m, n)
                run(dve, 0, NT - 1, lambda t: tile(t, True))
                tile(NT - 1, False)

            @block.tensor
            def _(pe):
                def pairs(i):
                    for b in (0, 1):
                        lin.product(pe, i, b)
                run(pe, 0, LEAD // 2, pairs)

                def tile(t):
                    for m in range(PLAIN):
                        lin.product(pe, first_pair(t) + m // 2, m % 2)
                    pe.wait_ge(s("gated"), t + 1)
                    pe.wait_ge(s("picked"), 2 * t + 2)
                    for n in range(3):
                        last = nc.tensor.transpose(ps_p[:, n, :], pick[:, n, :], ident[:])
                    last.then_inc(s("picks_turned"), 1)
                    for k in range(NBATCH):
                        m = PLAIN + k
                        lin.product(pe, first_pair(t) + m // 2, m % 2)
                        pe.wait_ge(s("onehot"), NBATCH * t + k + 1)
                        pe.wait_ge(s("oh1"), NBATCH * t + k + 1)
                        for half in (0, 1):
                            pe.wait_ge(s(f"gates_read{half}"), NBATCH * t + k)
                            for j in range(QB):
                                n = half * QB + j
                                last = nc.tensor.matmul(ps_w[half][:, j, :], o1[k % 2][:, n, :], o2[k % 2][:, n, :],
                                                        start=True, stop=True)
                            last.then_inc(s(f"gates_mm{half}"), 1)
                run(pe, 0, NT, tile)
                run(pe, (NK - TAIL) // 2, NK // 2, pairs)

        hidden.close()
        s.clear()

        with ExitStack() as c6:
            acc = sb(c6, "acc", [P, NT, D])
            with ExitStack() as c:
                v_raw = sb(c, "v_raw", [P, VG, D])
                v_hi = [sb(c, f"v_hi{b}", [P, VG, D], F32R) for b in (0, 1)]
                v_lo = [sb(c, f"v_lo{b}", [P, VG, D], F32R) for b in (0, 1)]
                w_raw = [sb(c, f"w_raw{b}", [P, N // WB, VG * WB]) for b in (0, 1)]
                g_act = [sb(c, f"g_act{b}", [P, VG, N]) for b in (0, 1)]
                a_hi = sb(c, "a_hi", [P, 2, VG, N], F32R)
                a_lo = sb(c, "a_lo", [P, 2, VG, N], F32R)
                ps_y = [pb(c, f"y_ps{b}", [P, 512]) for b in range(4)]
                npass = VGROUPS // 2
                block = c.enter_context(nc.Block())

                @block.sync
                def _(sp):
                    def step(i):
                        for gp in (0, 1):
                            sp.wait_ge(s("v_split"), VG * (2 * i + gp))
                            sp.dma_start(v_raw[:, :, :].rearrange("p c d -> p (c d)"),
                                         a["v"][:, bass.ds((2 * i + gp) * VG * D, VG * D)]
                                         ).then_inc(s("ld_v"), 16)
                            sp.wait_ge(s(f"a_split{gp}"), VG * i)
                            sp.dma_start(w_raw[gp][:], wgt_d[:, :, bass.ds((2 * i + gp) * VG * WB, VG * WB)]
                                         ).then_inc(s(f"ld_w{gp}"), 16)
                            sp.dma_start(g_act[gp][:], act_d[bass.ds((2 * i + gp) * VG, VG)].rearrange("c p n -> p c n")
                                         ).then_inc(s(f"ld_a{gp}"), 16)
                    run(sp, 0, npass, step)

                @block.scalar
                def _(act):
                    def step(i):
                        for gp in (0, 1):
                            act.wait_ge(s(f"y_mm{gp}"), 2 * NT * i)
                            act.wait_ge(s("ld_v"), 16 * (2 * i + gp) + 16)
                            for c_ in range(VG):
                                nc.scalar.activation(v_hi[gp][:, c_, :], v_raw[:, c_, :], ACT.Copy
                                                     ).then_inc(s("v_head"), 1)
                            for c_ in range(VG):
                                act.wait_ge(s(f"mult{gp}"), VG * i + c_ + 1)
                                nc.scalar.activation(a_hi[:, gp, c_, :], g_act[gp][:, c_, :], ACT.Copy
                                                     ).then_inc(s(f"a_head{gp}"), 1)
                    run(act, 0, npass, step)

                @block.gpsimd
                def _(pool):
                    def step(i):
                        for gp in (0, 1):
                            for c_ in range(VG):
                                pool.wait_ge(s("v_head"), VG * (2 * i + gp) + c_ + 1)
                                nc.gpsimd.tensor_tensor(v_lo[gp][:, c_, :], v_raw[:, c_, :],
                                                        v_hi[gp][:, c_, :].bitcast(F32), ALU.subtract
                                                        ).then_inc(s("v_split"), 1)
                    run(pool, 0, npass, step)

                @block.vector
                def _(dve):
                    nc.vector.memset(acc[:], 0.0).then_inc(s("acc0"), 1)
                    dve.wait_ge(s("acc0"), 1)

                    def prepare(i, gp):
                        dve.wait_ge(s(f"ld_w{gp}"), 16 * i + 16)
                        dve.wait_ge(s(f"ld_a{gp}"), 16 * i + 16)
                        for c_ in range(VG):
                            col = g_act[gp][:, c_, :].rearrange("p (b n) -> p b n", n=WB)
                            nc.vector.tensor_tensor(col, col, w_raw[gp][:, :, c_ * WB:c_ * WB + WB], ALU.mult
                                                    ).then_inc(s(f"mult{gp}"), 1)
                        for c_ in range(VG):
                            dve.wait_ge(s(f"a_head{gp}"), VG * i + c_ + 1)
                            nc.vector.tensor_tensor(a_lo[:, gp, c_, :], g_act[gp][:, c_, :],
                                                    a_hi[:, gp, c_, :].bitcast(F32), ALU.subtract
                                                    ).then_inc(s(f"a_split{gp}"), 1)

                    def add_up(i, gp):
                        for r in range(2 * NT):
                            q = 2 * NT * gp + r
                            dve.wait_ge(s(f"y_mm{gp}"), 2 * NT * i + r + 1)
                            sums = acc[:, r // 2, (r % 2) * 512:(r % 2) * 512 + 512]
                            nc.vector.tensor_tensor(sums, sums, ps_y[q % 4][:, :], ALU.add
                                                    ).then_inc(s(f"y_add{q % 4}"), 1)

                    def step(i, more=True):
                        prepare(i, 1)
                        add_up(i, 0)
                        if more:
                            prepare(i + 1, 0)
                        add_up(i, 1)
                    prepare(0, 0)
                    run(dve, 0, npass - 1, step)
                    step(npass - 1, more=False)

                @block.tensor
                def _(pe):
                    def step(i):
                        for gp in (0, 1):
                            pe.wait_ge(s(f"a_split{gp}"), VG * i + VG)
                            pe.wait_ge(s("v_split"), VG * (2 * i + gp) + VG)
                            for r in range(2 * NT):
                                q = 2 * NT * gp + r
                                ts = slice((r // 2) * P, (r // 2) * P + P)
                                ds_ = slice((r % 2) * 512, (r % 2) * 512 + 512)
                                pe.wait_ge(s(f"y_add{q % 4}"), 5 * i + q // 4)
                                for c_ in range(VG):
                                    hi, lo = a_hi[:, gp, c_, ts], a_lo[:, gp, c_, ts]
                                    nc.tensor.matmul(ps_y[q % 4][:, :], hi, v_hi[gp][:, c_, ds_], start=(c_ == 0), stop=False)
                                    nc.tensor.matmul(ps_y[q % 4][:, :], hi, v_lo[gp][:, c_, ds_], start=False, stop=False)
                                    last = nc.tensor.matmul(ps_y[q % 4][:, :], lo, v_hi[gp][:, c_, ds_],
                                                            start=False, stop=(c_ == VG - 1))
                                last.then_inc(s(f"y_mm{gp}"), 1)
                    run(pe, 0, npass, step)

            with ExitStack() as c:
                x2 = [sb(c, f"x2_{k}", [P, D]) for k in range(NT)]
                nf = sb(c, "nf", [P, D])
                ones = sb(c, "ones", [P, P])
                g2row = sb(c, "g2row", [P, 2, D])
                diag = sb(c, "diag", [P, 2 * KC, P])
                sqs = sb(c, "sqs", [P, D])
                st = sb(c, "st", [P, 5, NT])
                ps_g = pb(c, "ps_g", [P, 4, 512])
                block = c.enter_context(nc.Block())

                @block.sync
                def _(sp):
                    sp.dma_start(ones[:], a["ones"]).then_inc(s("ld_ones"), 16)
                    sp.dma_start(nf[:], a["norm_final"]).then_inc(s("ld7"), 16)
                    for k in range(NT):
                        sp.dma_start(x2[k][:], x2_d[k]).then_inc(s("ld7"), 16)
                    for k in range(NT):
                        sp.wait_ge(s("final"), k + 1)
                        dst = y_prompt if k == 0 else y_sample[(k - 1) * P:k * P, :]
                        sp.dma_start(dst, x2[k][:]).then_inc(s("st_y"), 16)
                    sp.wait_ge(s("st_y"), 16 * NT)

                @block.scalar
                def _(act):
                    for k in range(NT):
                        act.wait_ge(s("resid"), k + 1)
                        nc.scalar.activation(sqs[:], x2[k][:], ACT.Square, accum_out=st[:, 0, k:k + 1]
                                             ).then_inc(s("ssq"), 1)
                        act.wait_ge(s("ssq"), k + 1)
                    act.wait_ge(s("fin_var"), 1)
                    nc.scalar.activation(st[:, 2, :], st[:, 1, :], ACT.Sqrt).then_inc(s("fin_root"), 1)

                @block.vector
                def _(dve):
                    link = Chain(dve, s("dve7"))
                    V = nc.vector
                    for k in range(2 * KC):
                        V.tensor_scalar(diag[:, k, :], ident[:], mod[:, 5 * KC + k % KC, k // KC:k // KC + 1], None,
                                        ALU.mult).then_inc(s("diag"), 1)
                    for k in range(4):
                        dve.wait_ge(s("g2_ps"), k + 1)
                        link(V.tensor_copy(g2row[:, k // 2, (k % 2) * 512:(k % 2) * 512 + 512], ps_g[:, k, :]))
                    dve.wait_ge(s("ld7"), 16 * (NT + 1))
                    for k in range(NT):
                        link(V.tensor_tensor(acc[:, k, :], acc[:, k, :], g2row[:, min(k, 1), :], ALU.mult))
                        V.tensor_tensor(x2[k][:], x2[k][:], acc[:, k, :], ALU.add).then_inc(s("resid"), 1)
                    dve.wait_ge(s("ssq"), NT)
                    link(V.tensor_scalar(st[:, 0, :], st[:, 0, :], 1.0 / D, None, ALU.mult))
                    rstd_ops(dve, link, "fin", st[:, 0, :], st[:, 1, :], st[:, 1, :], st[:, 2, :], st[:, 3, :], st[:, 4, :])
                    for k in range(NT):
                        V.scalar_tensor_tensor(out=x2[k][:], in0=x2[k][:], scalar=st[:, 3, k:k + 1], in1=nf[:],
                                               op0=ALU.mult, op1=ALU.mult).then_inc(s("final"), 1)

                @block.tensor
                def _(pe):
                    pe.wait_ge(s("ld_ones"), 16)
                    for k in range(2 * KC):
                        pe.wait_ge(s("diag"), k + 1)
                        last = nc.tensor.matmul(ps_g[:, k // 4, (k % 4) * P:(k % 4) * P + P], ones[:], diag[:, k, :],
                                                start=True, stop=True)
                        if k % 4 == 3:
                            last.then_inc(s("g2_ps"), 1)


def layout(x):
    c = np.ascontiguousarray

    def columns(v):
        return np.asarray(v).reshape(-1, P).T

    def slabs(w, cols=None):
        w = np.asarray(w)
        w = w if cols is None else w[:, cols]
        k, m = w.shape
        return c(w.reshape(k // P, P, m // P, P).transpose(2, 1, 0, 3).reshape(m // P, P, k))

    x = {k: np.asarray(v) for k, v in x.items()}
    tokens = np.concatenate([x["x_prompt"][0], x["x_sample"][0]], 0)
    r = np.arange
    swapped = np.concatenate([r(ROPE // 2, ROPE), r(0, ROPE // 2)])
    kr0 = 384
    kr = np.concatenate([kr0 + r(ROPE), kr0 + swapped] * 2)
    order = np.concatenate([r(0, kr0), kr, r(kr0 + ROPE, x["w_in"].shape[2])])
    qh = r(HEADS)[:, None] * QK
    uq = x["w_uq"][0][:, np.concatenate([(qh + r(NOPE)).ravel(), (qh + NOPE + r(ROPE)).ravel(),
                                         (qh + NOPE + swapped).ravel()])]
    kh = r(HEADS)[:, None] * (NOPE + VD)
    ukv = x["w_ukv"][0][:, np.concatenate([(kh + r(NOPE)).ravel(), (kh + NOPE + r(VD)).ravel()])]
    out = {
        "x_t": tokens.T.reshape(KC, P, N).transpose(1, 0, 2),
        "cvec": np.stack([columns(x["c_ctx"]), columns(x["c"][0])], 2),
        "w_mod": slabs(x["w_mod"][0]), "bmod": columns(x["b_mod"][0]),
        "cols": np.concatenate([columns(x["norm_mix"][0]), columns(x["norm_ffn"][0]), columns(x["q_norm"][0]),
                                columns(x["kv_norm"][0]), columns(x["ret_gn"][0]),
                                np.tile(np.concatenate([x["ret_logit_fwd"][0], x["ret_logit_bwd"][0]]), (P, 1)),
                                np.tile(x["c_ctx"][:9], (P, 1))], 1),
        "w_in": slabs(x["w_in"][0], order),
        "w_uq": uq.reshape(2, P, D).transpose(1, 0, 2), "w_ukv": ukv.reshape(P, 2, 512),
        "cache_ckv_t": x["cache_ckv"][0, 0].T, "cache_kr_t": x["cache_krope"][0, 0].T,
        "state": np.stack([x["state_ret_fwd"][0, 0], x["state_ret_bwd"][0, 0]]).transpose(2, 0, 1, 3),
        "w_up": slabs(np.concatenate([x["w_up_a"][0], x["w_up_b"][0]], 0)),
        "w_o": slabs(x["w_o"][0]), "w_q": slabs(x["peer_wq"][0]),
        "keys_t": np.stack([x["peer_keys1"][0], x["peer_keys2"][0]], 1).reshape(16, NK, P).transpose(2, 0, 1),
        "u": x["peer_u"][0].reshape(NK, NK, KC, P).transpose(1, 3, 2, 0).reshape(NK, P, D),
        "v": x["peer_v"][0].reshape(NK, NK * D),
        "norm_final": np.tile(x["norm_final"], (P, 1)),
    }
    out.update(constants())
    return {k: c(v) for k, v in out.items()}


def constants():
    f = np.float32
    pos = np.arange(NLAT)
    freqs = np.power(f(ROPE_BASE), -np.arange(ROPE // 4, dtype=f) / f(ROPE // 4)).astype(f)
    ang = np.concatenate([(pos // GRID_W).astype(f)[:, None] * freqs, (pos % GRID_W).astype(f)[:, None] * freqs], 1)
    cos, sin = np.cos(ang).T.astype(f), np.sin(ang).T.astype(f)
    diff = (np.arange(NLAT + 384) - 384)[None, :] - np.arange(P)[:, None]
    p = np.arange(P, dtype=f)[:, None]
    full = lambda v: np.full((P, P), v, f)
    return {
        "cos_t": np.tile(np.concatenate([cos, cos], 0), (4, 1)), "sin_t": np.tile(np.concatenate([-sin, sin], 0), (4, 1)),
        "ident": np.eye(P, dtype=f), "ones": full(1.0), "inv_d": full(1.0 / D), "inv_q": full(1.0 / 256),
        "inv_k": full(1.0 / P),
        "rel0": np.maximum(diff, 0).astype(f), "rel1": np.maximum(-diff, 0).astype(f),
        "msk0": (diff >= 0).astype(f), "msk1": (diff <= 0).astype(f),
        "steps": np.tile(np.stack([np.arange(1, NLAT + 1), np.arange(NLAT, 0, -1)]).astype(f)[None], (P, 1, 1)),
        "ksteps": np.concatenate([np.repeat(P - 1 - p, RH, 1), np.repeat(p, RH, 1)], 1),
        "iota_r": np.tile(np.arange(NK, dtype=f), (P, 1)),
    }


OUTS = [("y_prompt", (NCTX, D)), ("y_sample", (NLAT, D)), ("new_ckv", (NCTX, 128)), ("new_kr", (NCTX, ROPE)),
        ("new_sf", (DK, RH, DK)), ("new_sb", (DK, RH, DK))]


def kernel(**inputs):
    import concourse.bacc as bacc
    from concourse.bass_utils import run_bass_kernel_spmd

    nc = bacc.Bacc("TRN2", target_bir_lowering=False, num_devices=1)
    arrays = layout(inputs)
    aps = {k: nc.dram_tensor(k + "_dram", v.shape, F32, kind="ExternalInput").ap() for k, v in arrays.items()}
    outs = [nc.dram_tensor(n + "_dram", shape, F32, kind="ExternalOutput").ap() for n, shape in OUTS]
    build(nc, aps, outs)
    result = run_bass_kernel_spmd(nc, [{k + "_dram": v for k, v in arrays.items()}], core_ids=[0])
    got = {n: result.results[0][n + "_dram"] for n, _ in OUTS}
    return (got["y_prompt"][None], got["y_sample"][None], got["new_ckv"][None, None], got["new_kr"][None, None],
            got["new_sf"].transpose(1, 0, 2)[None, None], got["new_sb"].transpose(1, 0, 2)[None, None])
```
